# Optimizing a Trainium2 kernel written in Bass

```python
import math
import jax, jax.numpy as jnp
from jax import lax
import numpy as np

D_MODEL = 1024
BATCH = 1
SEQ = 1024
DEPTH = 1

HEAD_DIM = 64
N_HEADS_A = 8
N_HEADS_B = 4
N_HEADS_MEM = 4
W_A = N_HEADS_A * HEAD_DIM
W_B = N_HEADS_B * HEAD_DIM
W_M = N_HEADS_MEM * HEAD_DIM
MIX_WIDTH = W_A + W_B + W_M
DILATED_PATTERNS = ((128, 1), (512, 4), (2048, 16))
N_IDX_HEADS = 8
IDX_DIM = 64
TOPK_MAX = 256
N_MEM = 256
Q_BLOCK = 128
RMS_EPS = 1e-6
SPLIT_SIZES = (W_A, W_A, W_A, W_B, HEAD_DIM, HEAD_DIM, W_M, MIX_WIDTH,
               N_IDX_HEADS * IDX_DIM, IDX_DIM, N_IDX_HEADS)
IN_COLS = W_A * 3 + W_B + 2 * HEAD_DIM + W_M + MIX_WIDTH + N_IDX_HEADS * IDX_DIM + IDX_DIM + N_IDX_HEADS

kernel_name = "hybrid_dilated_dsa_memory_block"

def rms_norm(x, g):
    x32 = x.astype(jnp.float32)
    y = x32 * lax.rsqrt(jnp.mean(x32 * x32, axis=-1, keepdims=True) + RMS_EPS)
    return (y * g.astype(jnp.float32)).astype(x.dtype)

def alibi_slopes(n):
    return 2.0 ** (-8.0 * jnp.arange(1, n + 1, dtype=jnp.float32) / n)

def dilated_band_attention(q, k, v, slopes, window, dilation):
    B, T, H, Dh = q.shape
    band = window // dilation
    n = T // dilation
    nb = -(-n // band)
    n_pad = nb * band

    def to_sub(a):
        a = a.reshape(B, n, dilation, H, Dh).transpose(0, 2, 3, 1, 4)
        a = jnp.pad(a, ((0, 0), (0, 0), (0, 0), (0, n_pad - n), (0, 0)))
        return a.reshape(B, dilation, H, nb, band, Dh)

    def with_prev(a):
        prev = jnp.pad(a, ((0, 0), (0, 0), (0, 0), (1, 0), (0, 0), (0, 0)))[:, :, :, :-1]
        return jnp.concatenate([prev, a], axis=4)

    qs = to_sub(q)
    kb = with_prev(to_sub(k))
    vb = with_prev(to_sub(v))
    s = jnp.einsum('brhnqc,brhnkc->brhnqk', qs, kb).astype(jnp.float32) * (Dh ** -0.5)
    qi = jnp.arange(band)[:, None]
    ki = jnp.arange(2 * band)[None, :]
    dist = band + qi - ki
    blk = jnp.arange(nb)[:, None, None]
    valid = (dist >= 0) & (dist <= band) & (blk * band + ki - band >= 0)
    bias = -slopes[:, None, None, None] * (dist * dilation).astype(jnp.float32)[None, None]
    s = jnp.where(valid, s + bias, -jnp.inf)
    m = jnp.max(s, axis=-1, keepdims=True)
    p = jnp.exp(s - m)
    l = jnp.sum(p, axis=-1, keepdims=True)
    o = jnp.einsum('brhnqk,brhnkc->brhnqc', p.astype(vb.dtype), vb).astype(jnp.float32) / l
    lse = (m + jnp.log(l))[..., 0]
    o = o.reshape(B, dilation, H, n_pad, Dh)[:, :, :, :n].transpose(0, 3, 1, 2, 4).reshape(B, T, H, Dh)
    lse = lse.reshape(B, dilation, H, n_pad)[..., :n].transpose(0, 3, 1, 2).reshape(B, T, H)
    return o, lse

def dilated_mixture_attention(q, k, v, slopes):
    outs, lses = [], []
    for window, dilation in DILATED_PATTERNS:
        o, lse = dilated_band_attention(q, k, v, slopes, window, dilation)
        outs.append(o)
        lses.append(lse)
    wts = jax.nn.softmax(jnp.stack(lses, axis=0), axis=0)
    return jnp.sum(wts[..., None] * jnp.stack(outs, axis=0), axis=0)

def dsa_attention(qB, kB, vB, qI, kI, wI, slopes):
    B, T, H, Dh = qB.shape
    k_sel = min(TOPK_MAX, T // 4)
    nblk = T // Q_BLOCK
    pos = jnp.arange(T)

    def blocks(a):
        return a.reshape(B, nblk, Q_BLOCK, *a.shape[2:]).swapaxes(0, 1)

    def one_block(args):
        qb, qib, wib, tq = args
        logits = jnp.einsum('bqhc,bsc->bqhs', qib, kI).astype(jnp.float32) * (IDX_DIM ** -0.5)
        score = jnp.einsum('bqh,bqhs->bqs', wib.astype(jnp.float32) * (N_IDX_HEADS ** -0.5),
                           jax.nn.relu(logits))
        causal = pos[None, :] <= tq[:, None]
        score = jnp.where(causal, score, -jnp.inf)
        _, idx = lax.top_k(score, k_sel)
        gather = jax.vmap(lambda kv, ii: kv[ii])
        k_g = gather(kB, idx)
        v_g = gather(vB, idx)
        s = jnp.einsum('bqhc,bqkc->bhqk', qb, k_g).astype(jnp.float32) * (Dh ** -0.5)
        dist = (tq[:, None] - idx).astype(jnp.float32)
        s = s - slopes[None, :, None, None] * dist[:, None]
        admissible = (idx <= tq[:, None])[:, None]
        s = jnp.where(admissible, s, -jnp.inf)
        p = jax.nn.softmax(s, axis=-1)
        return jnp.einsum('bhqk,bqkc->bqhc', p.astype(v_g.dtype), v_g)

    out = lax.map(one_block, (blocks(qB), blocks(qI), blocks(wI), pos.reshape(nblk, Q_BLOCK)))
    return out.swapaxes(0, 1).reshape(B, T, H, Dh)

def memory_attention(q, k, v):
    s = jnp.einsum('bthc,bmhc->bhtm', q, k).astype(jnp.float32) * (q.shape[-1] ** -0.5)
    p = jax.nn.softmax(s, axis=-1)
    return jnp.einsum('bhtm,bmhc->bthc', p.astype(v.dtype), v)

def setup_inputs(seed: int = 0) -> dict:
    key = jax.random.key(seed)
    ks = jax.random.split(key, 8)
    f32 = jnp.float32
    x = jax.random.normal(ks[0], (BATCH, SEQ, D_MODEL), f32)
    mem = jax.random.normal(ks[1], (BATCH, N_MEM, D_MODEL), f32)
    g_in = 1.0 + 0.01 * jax.random.normal(ks[2], (DEPTH, D_MODEL), f32)
    g_mem = 1.0 + 0.01 * jax.random.normal(ks[3], (DEPTH, D_MODEL), f32)
    w_in = jax.random.normal(ks[4], (DEPTH, D_MODEL, IN_COLS), f32) * (D_MODEL ** -0.5)
    w_mem_kv = jax.random.normal(ks[5], (DEPTH, D_MODEL, 2 * W_M), f32) * (D_MODEL ** -0.5)
    w_out = jax.random.normal(ks[6], (DEPTH, MIX_WIDTH, D_MODEL), f32) * (MIX_WIDTH ** -0.5)
    g_final = 1.0 + 0.01 * jax.random.normal(ks[7], (D_MODEL,), f32)
    return {"x": x, "mem": mem, "g_in": g_in, "g_mem": g_mem, "w_in": w_in,
            "w_mem_kv": w_mem_kv, "w_out": w_out, "g_final": g_final}

def reference(x, mem, g_in, g_mem, w_in, w_mem_kv, w_out, g_final):
    B, T, _ = x.shape
    split_points = np.cumsum(np.array(SPLIT_SIZES))[:-1].tolist()
    slopes_a = alibi_slopes(N_HEADS_A)
    slopes_b = alibi_slopes(N_HEADS_B)
    for layer in range(DEPTH):
        h = rms_norm(x, g_in[layer])
        proj = h @ w_in[layer]
        qA, kA, vA, qB, kB, vB, qM, gate, qI, kI, wI = jnp.split(proj, split_points, axis=-1)
        qA = qA.reshape(B, T, N_HEADS_A, HEAD_DIM)
        kA = kA.reshape(B, T, N_HEADS_A, HEAD_DIM)
        vA = vA.reshape(B, T, N_HEADS_A, HEAD_DIM)
        qB = qB.reshape(B, T, N_HEADS_B, HEAD_DIM)
        qM = qM.reshape(B, T, N_HEADS_MEM, HEAD_DIM)
        qI = qI.reshape(B, T, N_IDX_HEADS, IDX_DIM)

        mem_n = rms_norm(mem, g_mem[layer])
        kvM = mem_n @ w_mem_kv[layer]
        kM, vM = jnp.split(kvM, 2, axis=-1)
        kM = kM.reshape(B, -1, N_HEADS_MEM, HEAD_DIM)
        vM = vM.reshape(B, -1, N_HEADS_MEM, HEAD_DIM)

        oA = dilated_mixture_attention(qA, kA, vA, slopes_a)
        oB = dsa_attention(qB, kB, vB, qI, kI, wI, slopes_b)
        oM = memory_attention(qM, kM, vM)

        o = jnp.concatenate([oA.astype(x.dtype).reshape(B, T, W_A),
                             oB.astype(x.dtype).reshape(B, T, W_B),
                             oM.astype(x.dtype).reshape(B, T, W_M)], axis=-1)
        o = o * jax.nn.silu(gate)
        x = x + o @ w_out[layer]
    return rms_norm(x, g_final)


_drawn_inputs = setup_inputs


def setup_inputs(seed=0):
    import zlib

    import numpy as np

    out = dict(_drawn_inputs(seed))
    spreads = {}
    factors = {'g_in': 4.214, 'g_mem': 8.0, 'g_final': 5.722}
    for name, (base, spread) in spreads.items():
        noise = np.random.default_rng([zlib.crc32(name.encode()), seed]).standard_normal(out[name].shape)
        drawn = base * np.exp(spread * noise) if base else spread * noise
        out[name] = __import__('jax').numpy.asarray(drawn.astype(out[name].dtype))
    for name, factor in factors.items():
        out[name] = (out[name] * factor).astype(out[name].dtype)
    return out
```

```python
import math
from contextlib import ExitStack

import numpy as np

import concourse.bass as bass
from concourse import mybir

F32 = mybir.dt.float32
F32R = mybir.dt.float32r
ALU = mybir.AluOpType
ACT = mybir.ActivationFunctionType
AX_X = mybir.AxisListType.X

P = 128
T = 1024
D = 1024
KD = D // P
NT = T // P
N_MEM = 256
MT = N_MEM // P
DH = 64
HALF = 512
H_A, H_B, H_M, H_I = 8, 4, 4, 8
TOPK = 256
FIRST_TOPK = TOPK // P
EPS = 1e-6
BIG = 1e30

C_QA, C_KA, C_VA = 0, 512, 1024
C_QB = 1536
C_KB = C_QB + H_B * DH
C_VB = C_KB + DH
C_QM = C_VB + DH
C_GATE = C_QM + H_M * DH
C_QI = C_GATE + 1024
C_KI = C_QI + H_I * DH
C_WI = C_KI + DH

PAIRS = [("M", 0, 6), ("M", 1, 7), ("A", 0, 0), ("A", 1, 1), ("A", 2, 2), ("A", 3, 3), ("B", 0, 4), ("B", 1, 5)]
NP = len(PAIRS)
STEPS = NP * NT


def w_tiles():
    out = [("kIB", None, [(C_KI, DH), (C_KB, DH)])]
    out += [("qI", j, [(C_QI + P * j, P)]) for j in range(H_I // 2)]
    out += [("vBwI", None, [(C_VB, DH), (C_WI, H_I)])]
    for p, (g, j, f) in enumerate(PAIRS):
        if g == "A":
            out += [("k", p, [(C_KA + P * j, P)]), ("v", p, [(C_VA + P * j, P)])]
        out += [("q", p, [({"A": C_QA, "B": C_QB, "M": C_QM}[g] + P * j, P)]), ("gate", p, [(C_GATE + P * f, P)])]
    return out


W_TILES = w_tiles()
FIRST_W = {p: min(n for n, w in enumerate(W_TILES) if w[1] == p and w[0] not in ("qI",)) for p in range(NP)}
N_W = len(W_TILES)


def width(w):
    return sum(n for _, n in W_TILES[w][2])


def pair_of_step(s):
    return s // NT, s % NT


def key_tiles(s):
    p, i = pair_of_step(s)
    return MT if PAIRS[p][0] == "M" else i + 1


def chunks(s):
    n = key_tiles(s)
    return [range(c, min(c + 4, n)) for c in range(0, n, 4)]


CHUNK0 = [sum(len(chunks(q)) for q in range(s)) for s in range(STEPS + 1)]


def projection_of_step(s):
    p, i = pair_of_step(s)
    if p + 1 < NP:
        w = FIRST_W[p + 1] + i // 2
        if w < N_W and W_TILES[w][1] == p + 1:
            return w, i % 2
    return None


def v_turn_of_step(s):
    p, i = pair_of_step(s)
    if p + 1 < NP and PAIRS[p + 1][0] == "A" and i in (3, 4):
        return p + 1, i - 3
    return None


PRE_W = FIRST_W[1]
IDX_TILES = list(range(FIRST_TOPK, NT))
IDX_UNITS = [(i, h) for i in IDX_TILES for h in range(H_I)]
X_OFF = {i: sum(P * (q + 1) for q in range(FIRST_TOPK, i)) for i in IDX_TILES}
X_COLS = sum(P * (q + 1) for q in IDX_TILES)
PRE_PAIR_HALVES = [(w, b) for w in range(FIRST_W[0], FIRST_W[1]) for b in range(2)]
ROUNDS = TOPK // 8
HALVINGS = 12
NEVER = -3e38
CHOICE_SLOTS = [[q for q in range(HALVINGS + 5) if q * 2 * (NT - 1) // (HALVINGS + 5) == n] for n in range(2 * (NT - 1))]


def build_program(nc, x, mem, g_in, g_mem, w_in, w_mem, w_out, g_final, dist_tab, a_tab, out):
    with ExitStack() as ctx:
        def sb(name, shape, dt=F32):
            return ctx.enter_context(nc.sbuf_tensor(name, shape, dt))

        def sem(name):
            return ctx.enter_context(nc.semaphore(name))

        h_hi = sb("h_hi", [P, KD, T], F32R)
        h_lo = sb("h_lo", [P, KD, T], F32R)
        w_hl = sb("w_hl", [P, 2, 2, KD, P], F32R)
        w_raw = sb("w_raw", [P, KD, P])
        q_sb = sb("q_sb", [P, 2, T])
        k_sb = sb("k_sb", [P, 2, T])
        v_sb = sb("v_sb", [P, 2, NT, P])
        vT = sb("vT", [P, HALF])
        gate = sb("gate", [P, 2, T])
        v_b = sb("v_b", [P, NT, DH])
        w_i = sb("w_i", [P, NT, H_I])
        k_b = sb("k_b", [P, T])
        bias = sb("bias", [P, 2, T])
        prob = sb("prob", [P, 2, 2, T])
        probT = sb("probT", [P, 2, 2, 4, P])
        idx = sb("idx", [P, X_COLS])
        og = sb("og", [P, 6, T])
        dist = sb("dist", [P, T])
        ident = sb("ident", [P, P])
        lsum = sb("lsum", [P, 2, NT, 2])
        linv = sb("linv", [P, 4, 2, DH])
        nmax = sb("nmax", [P, 2, 2])
        picked = sb("picked", [P, T])
        cut8 = sb("cut8", [P, 3, 8])
        eight = sb("eight", [P, 8])
        tk = sb("tk", [P, 8])
        reach = sb("reach", [P, len(IDX_TILES)])
        failed = sb("failed", [P, 1], mybir.dt.int32)
        stat = sb("stat", [P, 5, MT + NT])
        ogf = og[:, :, :].rearrange("p a t -> p (a t)")
        q_i = ogf[:, 0:4 * T].rearrange("p (a t) -> p a t", a=4)
        k_i = ogf[:, 4 * T:5 * T]
        x_raw = [og[:, r, :] for r in range(6)] + [q_sb[:, 0, :], q_sb[:, 1, :], k_sb[:, 0, :], k_sb[:, 1, :]]
        x_scaled = [prob[:, 0, 0, :], prob[:, 0, 1, :]]
        g_row, gm_row = prob[:, 1, 0, :], prob[:, 1, 1, :]
        memT = v_sb[:, :, :, :].rearrange("p a b c -> p (a b c)").rearrange("p (k m) -> p k m", k=KD)
        wm_raw = probT[:, :, :, :, :].rearrange("p a b c d -> p (a b c d)").rearrange("p (a k m) -> p a k m", a=2, k=KD)
        relu = [prob[:, 0, 0, :], prob[:, 0, 1, :], prob[:, 1, 0, :], prob[:, 1, 1, :]]
        k_m = bias[:, 0, 0:2 * N_MEM].rearrange("p (a m) -> p a m", a=2)
        v_m = bias[:, 0, 2 * N_MEM:4 * N_MEM].rearrange("p (t f) -> p t f", t=MT)
        vmT = vT[:, 0:2 * N_MEM].rearrange("p (a m) -> p a m", a=2)
        wo_hi, wo_lo = h_hi, h_lo
        x_res = [prob[:, 0, 0, :], prob[:, 0, 1, :]]
        y_row = [prob[:, 1, 0, :], prob[:, 1, 1, :]]
        gf_row = bias[:, 0, :]
        sq_junk = bias[:, 1, :]

        def og_of(p):
            return og[:, p, :] if p < 6 else k_sb[:, p - 6, :]

        s_ps = [ctx.enter_context(nc.psum_tensor(f"s_ps{a}", [P, T], F32)) for a in range(2)]
        pt_ps = [ctx.enter_context(nc.psum_tensor(f"pt_ps{a}", [P, 4, P], F32)) for a in range(2)]
        o_ps = ctx.enter_context(nc.psum_tensor("o_ps", [P, HALF], F32))
        j_ps = ctx.enter_context(nc.psum_tensor("j_ps", [P, HALF], F32))
        j_banks = [j_ps, o_ps]
        turn_banks = [s_ps[0][:, 0:HALF], s_ps[0][:, HALF:T], s_ps[1][:, 0:HALF], s_ps[1][:, HALF:T],
                      pt_ps[0][:, :, :].rearrange("p a b -> p (a b)"), pt_ps[1][:, :, :].rearrange("p a b -> p (a b)")]

        x_in = [sem(f"x_in{r}") for r in range(MT + NT)]
        rows_in = sem("rows_in")
        consts_in = sem("consts_in")
        ident_ready = sem("ident_ready")
        eight_ready = sem("eight_ready")
        squares_ready = sem("squares_ready")
        var_ready = sem("var_ready")
        root_ready = sem("root_ready")
        x_ready = sem("x_ready")
        turned = sem("turned")
        hi_ready = sem("hi_ready")
        lo_ready = sem("lo_ready")
        wm_in = [sem("wm_in0"), sem("wm_in1")]
        w_in_sem = sem("w_in_sem")
        w_hi_ready = sem("w_hi_ready")
        w_lo_ready = sem("w_lo_ready")
        j_done = sem("j_done")
        j_free = sem("j_free")
        gate_ready = sem("gate_ready")
        idx_scored = sem("idx_scored")
        relu_ready = sem("relu_ready")
        idx_added = sem("idx_added")
        reach_ready = sem("reach_ready")
        idx_masked = sem("idx_masked")
        spoiled = sem("spoiled")
        spoiled_any = sem("spoiled_any")
        topk_done = sem("topk_done")
        half_mask = sem("half_mask")
        mask_ready = sem("mask_ready")
        bias_in = sem("bias_in")
        bias_ready = [sem("bias_ready_a"), sem("bias_ready_b")]
        scored = [sem("scored_a"), sem("scored_b")]
        biased = [sem("biased_a"), sem("biased_b")]
        prob_ready = [sem("prob_ready_a"), sem("prob_ready_b")]
        pt_done = [sem("pt_done_a"), sem("pt_done_b")]
        pt_ready = [sem("pt_ready_a"), sem("pt_ready_b")]
        pv_done = sem("pv_done")
        linv_ready = sem("linv_ready")
        linv_turned = sem("linv_turned")
        linv_used = sem("linv_used")
        og_ready = sem("og_ready")
        wo_in = sem("wo_in")
        wo_hi_ready = sem("wo_hi_ready")
        wo_lo_ready = sem("wo_lo_ready")
        gf_in = sem("gf_in")
        xr_in = [sem("xr_in0"), sem("xr_in1")]
        og_hi_ready = sem("og_hi_ready")
        og_lo_ready = sem("og_lo_ready")
        out_done = sem("out_done")
        y_ready = sem("y_ready")
        ysq_ready = sem("ysq_ready")
        yvar_ready = sem("yvar_ready")
        yroot_ready = sem("yroot_ready")
        y_final = sem("y_final")
        stored = [sem("stored0"), sem("stored1")]
        dve_seq = sem("dve_seq")

        x_t = x.rearrange("b (t p) d -> (b t) p d", p=P)
        mem_t = mem.rearrange("b (t p) d -> (b t) p d", p=P)
        w_k = w_in.rearrange("l (k p) c -> (l p) k c", p=P)
        wm_k = w_mem.rearrange("l (k p) c -> (l p) k c", p=P)
        wo_k = w_out.rearrange("l (f p) c -> (l f) p c", p=P)
        out_t = out.rearrange("b (t p) d -> (b t) p d", p=P)

        def dist_slice(i):
            return dist[:, T - P * (i + 1):T]

        def x_slice(i):
            return idx[:, X_OFF[i]:X_OFF[i] + P * (i + 1)]

        def dist_of(i):
            return dist_slice(i) if i < FIRST_TOPK else x_slice(i)

        uses = [("mem", w, 0) for w in range(4)] + [("memturn", 0, 0)]
        uses += [("w", w, b) for w in range(FIRST_W[0] - 1) for b in range(2)]
        uses += [(kind, w, b) for b in range(2) for kind, w in (("w", FIRST_W[0] - 1), ("bturn", 0))]
        uses += [("w", w, b) for w, b in PRE_PAIR_HALVES]
        n_pre = len(uses)
        for s in range(STEPS):
            if v_turn_of_step(s):
                uses.append(("vturn", *v_turn_of_step(s)))
            if projection_of_step(s):
                uses.append(("w", *projection_of_step(s)))
        use_number = {u: m for m, u in enumerate(uses)}

        def bank_of(m):
            return j_banks[m % 2] if m < n_pre else j_ps

        def free_before(m):
            return m - 1 if m < n_pre else m

        def evacuated(p, what, b=1):
            w = next(n for n, t in enumerate(W_TILES) if t[0] == what and t[1] == p)
            return use_number[("w", w, b)] + 1

        def projected(w):
            return use_number[("w", w, 1)] + 1

        block = ctx.enter_context(nc.Block())

        @block.sync
        def _(sp):
            sp.dma_start(x_raw[0], mem_t[0]).then_inc(x_in[0], 16)
            sp.dma_start(x_raw[1], mem_t[1]).then_inc(x_in[1], 16)
            sp.dma_start(gm_row, g_mem.broadcast_to([P, D])).then_inc(rows_in, 16)
            sp.dma_start(wm_raw[:, 0], wm_k[:, :, 0:P]).then_inc(wm_in[0], 16)
            for t in range(4):
                sp.dma_start(x_raw[MT + t], x_t[t]).then_inc(x_in[MT + t], 16)
            sp.dma_start(g_row, g_in.broadcast_to([P, D])).then_inc(rows_in, 16)

            def load_w(w):
                if w:
                    sp.wait_ge(w_hi_ready, w)
                    sp.wait_ge(w_lo_ready, w)
                at = 0
                for c, n in W_TILES[w][2]:
                    sp.dma_start(w_raw[:, :, at:at + n], w_k[:, :, c:c + n]).then_inc(w_in_sem, 16)
                    at += n

            load_w(0)
            sp.dma_start(wm_raw[:, 1], wm_k[:, :, P:2 * P]).then_inc(wm_in[1], 16)
            for t in range(4, NT):
                sp.dma_start(x_raw[MT + t], x_t[t]).then_inc(x_in[MT + t], 16)
            sp.dma_start(dist[:, :], dist_tab).then_inc(consts_in, 16)
            load_w(1)
            for w in range(2, 4):
                sp.wait_ge(j_done, w - 1)
                sp.dma_start(wm_raw[:, w % 2], wm_k[:, :, P * w:P * w + P]).then_inc(wm_in[w % 2], 16)
            n_a = 0
            next_w = 2
            for s in range(-1, STEPS):
                p, i = pair_of_step(s) if s >= 0 else (-1, 0)
                ahead = (projection_of_step(s)[0] + 2) if s >= 0 and projection_of_step(s) else 0
                if s < 0:
                    ahead = PRE_W + 1
                while next_w < min(ahead, N_W):
                    load_w(next_w)
                    next_w += 1
                if i == 0 and s >= 0 and PAIRS[p][0] == "A":
                    for a in range(2):
                        sp.wait_ge(biased[a], s)
                        if PAIRS[p - 1][0] == "M":
                            sp.wait_ge(pv_done, CHUNK0[s])
                        sp.dma_start(bias[:, a, :], a_tab[2 * PAIRS[p][1] + a]).then_inc(bias_in, 16)
                    n_a += 1
            while next_w < N_W:
                load_w(next_w)
                next_w += 1
            for p in range(NP):
                sp.wait_ge(w_hi_ready if p == 0 else wo_hi_ready, N_W if p == 0 else p)
                sp.wait_ge(w_lo_ready if p == 0 else wo_lo_ready, N_W if p == 0 else p)
                sp.dma_start(w_raw[:, :, :].rearrange("p k m -> p (k m)"), wo_k[PAIRS[p][2]]).then_inc(wo_in, 16)
            for a in range(2):
                sp.wait_ge(biased[a], STEPS)
            sp.dma_start(gf_row, g_final.unsqueeze(0).broadcast_to([P, D])).then_inc(gf_in, 16)
            for a in range(2):
                sp.wait_ge(pt_done[a], CHUNK0[STEPS])
            for t in range(NT):
                if t >= 2:
                    sp.wait_ge(y_ready, t - 1)
                sp.dma_start(x_res[t % 2], x_t[t]).then_inc(xr_in[t % 2], 16)
                if t >= 1:
                    sp.wait_ge(y_final, t)
                    sp.dma_start(out_t[t - 1], y_row[(t - 1) % 2]).then_inc(stored[(t - 1) % 2], 16)
            sp.wait_ge(y_final, NT)
            sp.dma_start(out_t[NT - 1], y_row[(NT - 1) % 2]).then_inc(stored[(NT - 1) % 2], 16)
            for b in range(2):
                sp.wait_ge(stored[b], 16 * NT // 2)

        @block.gpsimd
        def _(pool):
            pool.memset(ident[:, :], 0.0).then_inc(ident_ready, 1)
            pool.wait_ge(ident_ready, 1)
            pool.affine_select(out=ident[:, :], in_=ident[:, :], compare_op=ALU.not_equal, fill=1.0, base=0,
                               pattern=[[-1, P]], channel_multiplier=1).then_inc(ident_ready, 1)

            def split_lo(w):
                pool.wait_ge(w_hi_ready, w + 1)
                n = width(w)
                pool.tensor_tensor(w_hl[:, w % 2, 1, :, 0:n], w_raw[:, :, 0:n],
                                   w_hl[:, w % 2, 0, :, 0:n].bitcast(F32), ALU.subtract).then_inc(w_lo_ready, 1)

            pool.iota(eight[:, :], pattern=[[1, 8]], base=0, channel_multiplier=0,
                      allow_small_or_imprecise_dtypes=True).then_inc(eight_ready, 1)
            for w in range(PRE_W):
                split_lo(w)
            for n, i in enumerate(IDX_TILES):
                pool.wait_ge(reach_ready, n + 1)
                diagonal = x_slice(i)[:, P * i:P * (i + 1)]
                pool.affine_select(out=diagonal, in_=diagonal, compare_op=ALU.is_ge, fill=-BIG, base=0,
                                   pattern=[[-1, P]], channel_multiplier=1).then_inc(idx_masked, 1)
            pool.wait_ge(consts_in, 16)
            next_w = PRE_W
            masks = 0
            for s in range(STEPS):
                p, i = pair_of_step(s)
                ahead = (projection_of_step(s)[0] + 2) if projection_of_step(s) else 0
                if PAIRS[p][0] == "B":
                    if i >= FIRST_TOPK:
                        pool.wait_ge(mask_ready, i - FIRST_TOPK + 1)
                    for a in range(2):
                        slope = 2.0 ** (-8.0 * (2 * PAIRS[p][1] + a + 1) / H_B)
                        pool.wait_ge(biased[a], s)
                        pool.tensor_scalar(bias[:, a, 0:P * (i + 1)], dist_of(i), slope, 0.0,
                                           ALU.mult, ALU.add).then_inc(bias_ready[a], 1)
                if i == 0 and 1 <= p <= len(IDX_TILES):
                    pool.wait_ge(spoiled, p)
                    pool.partition_all_reduce(failed[:, :], tk[:, 5:6], P, bass.bass_isa.ReduceOp.add)\
                        .then_inc(spoiled_any, 1)
                if i == 1 and 1 <= p <= len(IDX_TILES):
                    t = IDX_TILES[p - 1]
                    n = P * (t + 1)
                    pool.wait_ge(topk_done, p)
                    pool.tensor_scalar(x_slice(t), picked[:, n - 1::-1], -2e38, BIG,
                                       ALU.is_le, ALU.mult).then_inc(half_mask, 1)
                    masks += 1
                    pool.wait_ge(half_mask, masks)
                    pool.tensor_tensor(x_slice(t), x_slice(t), dist_slice(t), ALU.add).then_inc(mask_ready, 1)
                while next_w < min(ahead, N_W):
                    split_lo(next_w)
                    next_w += 1
                if (p, i) >= (NP - 2, 4):
                    n = (p - NP + 2) * NT + i - 4
                    if n < NP:
                        pool.wait_ge(wo_hi_ready, n + 1)
                        pool.tensor_tensor(wo_lo[:, n, :], w_raw[:, :, :].rearrange("p k m -> p (k m)"),
                                           wo_hi[:, n, :].bitcast(F32), ALU.subtract).then_inc(wo_lo_ready, 1)
            for t in range(NT):
                pool.wait_ge(og_hi_ready, t + 1)
                cut = slice(P * t, P * t + P)
                pool.tensor_tensor(w_hl[:, t % 2, 1, 0:6, :], og[:, :, cut],
                                   w_hl[:, t % 2, 0, 0:6, :].bitcast(F32), ALU.subtract)
                pool.tensor_tensor(w_hl[:, t % 2, 1, 6:8, :], k_sb[:, :, cut],
                                   w_hl[:, t % 2, 0, 6:8, :].bitcast(F32), ALU.subtract).then_inc(og_lo_ready, 1)

        @block.scalar
        def _(act):

            def square_sums(rs):
                for r in rs:
                    act.wait_ge(x_in[r], 16)
                    if r >= 2:
                        act.wait_ge(squares_ready, r - 1)
                    act.activation(gate[:, r % 2, :], x_raw[r], ACT.Square,
                                   accum_out=stat[:, 0, r:r + 1]).then_inc(squares_ready, 1)

            def root(n, a, b):
                act.wait_ge(var_ready, n + 1)
                act.activation(stat[:, 2, a:b], stat[:, 1, a:b], ACT.Sqrt).then_inc(root_ready, 1)

            def split_hi(w):
                act.wait_ge(w_in_sem, 16 * sum(len(W_TILES[q][2]) for q in range(w + 1)))
                if w >= 2:
                    act.wait_ge(j_done, projected(w - 2))
                n = width(w)
                act.activation(w_hl[:, w % 2, 0, :, 0:n], w_raw[:, :, 0:n], ACT.Copy).then_inc(w_hi_ready, 1)

            def evacuate(m):
                kind, w, b = uses[m]
                bank = bank_of(m)
                act.wait_ge(j_done, m + 1)
                cut = slice(HALF * b, HALF * b + HALF)
                if kind == "mem":
                    dst = k_m[:, w, :] if w < 2 else vmT[:, w - 2, :]
                    last = act.activation(dst, bank[:, 0:N_MEM], ACT.Copy)
                elif kind == "memturn":
                    last = act.activation(v_m, bank[:, :].rearrange("p (t f) -> p t f", t=MT), ACT.Copy)
                elif kind == "bturn":
                    src = bank[:, 0:4 * 72].rearrange("p (t c) -> p t c", t=4)
                    act.activation(v_b[:, 4 * b:4 * b + 4, :], src[:, :, 0:DH], ACT.Copy)
                    last = act.activation(w_i[:, 4 * b:4 * b + 4, :], src[:, :, DH:DH + H_I], ACT.Copy,
                                          scale=float(H_I) ** -0.5)
                elif kind == "vturn":
                    last = act.activation(v_sb[:, w % 2, 4 * b:4 * b + 4, :].rearrange("p t f -> p (t f)"),
                                          bank[:, :], ACT.Copy)
                else:
                    what, p, _ = W_TILES[w]
                    if what == "kIB":
                        act.activation(k_i[0:DH, cut], bank[0:DH, :], ACT.Copy)
                        act.activation(k_i[DH:P, cut], bank[0:DH, :], ACT.Copy)
                        act.activation(k_b[0:DH, cut], bank[DH:P, :], ACT.Copy)
                        last = act.activation(k_b[DH:P, cut], bank[DH:P, :], ACT.Copy)
                    elif what == "qI":
                        last = act.activation(q_i[:, p, cut], bank[:, :], ACT.Copy, scale=DH ** -0.5)
                    elif what == "vBwI":
                        last = act.activation(vT[0:72, :], bank[0:72, :], ACT.Copy)
                    elif what == "k":
                        last = act.activation(k_sb[:, p % 2, cut], bank[:, :], ACT.Copy)
                    elif what == "v":
                        last = act.activation(vT[:, :], bank[:, :], ACT.Copy)
                    elif what == "q":
                        last = act.activation(q_sb[:, p % 2, cut], bank[:, :], ACT.Copy, scale=-(DH ** -0.5))
                    else:
                        last = act.activation(gate[:, p % 2, cut], bank[:, :], ACT.Copy)
                last.then_inc(j_free, 1)
                if kind == "w" and W_TILES[w][0] == "gate" and b == 1:
                    p = W_TILES[w][1]
                    act.wait_ge(j_free, m + 1)
                    act.activation(gate[:, p % 2, :], gate[:, p % 2, :], ACT.Silu).then_inc(gate_ready, 1)

            square_sums(range(0, MT))
            root(0, 0, MT)
            split_hi(0)
            square_sums(range(MT, MT + 4))
            root(1, MT, MT + 4)

            def high(u):
                r, b = u // 2, u % 2
                act.wait_ge(turned, u + 1)
                src = turn_banks[u % 6].rearrange("p (k t) -> p k t", k=4)
                if r < MT:
                    dst = memT[:, 4 * b:4 * b + 4, P * r:P * r + P]
                else:
                    dst = h_hi[:, 4 * b:4 * b + 4, P * (r - MT):P * (r - MT) + P]
                act.activation(dst, src, ACT.Copy).then_inc(hi_ready, 1)

            for u in range(2 * MT):
                high(u)
            square_sums(range(MT + 4, MT + NT))
            root(2, MT + 4, MT + NT)
            m = 0
            for _ in range(5):
                evacuate(m)
                m += 1
            for u in range(2 * MT, 2 * (MT + NT)):
                high(u)
            for w in range(FIRST_W[0]):
                split_hi(w + 1)
                for _ in range(2 if w + 1 < FIRST_W[0] else 4):
                    evacuate(m)
                    m += 1
            for u, (i, h) in enumerate(IDX_UNITS):
                if h == 0 and i - FIRST_TOPK < len(PRE_PAIR_HALVES):
                    w, b = PRE_PAIR_HALVES[i - FIRST_TOPK]
                    if b == 0 and w + 1 < PRE_W:
                        split_hi(w + 1)
                    evacuate(m)
                    m += 1
                act.wait_ge(idx_scored, u + 1)
                if u >= 4:
                    act.wait_ge(idx_added, u - 3)
                n = P * (i + 1)
                act.activation(relu[u % 4][:, 0:n], s_ps[u % 2][:, 0:n], ACT.Relu).then_inc(relu_ready, 1)
            next_w = PRE_W

            def copy_probT(s, c):
                g = CHUNK0[s] + c
                act.wait_ge(pt_done[0], g + 1)
                if g >= 2:
                    act.wait_ge(pv_done, g - 1)
                n = len(chunks(s)[c])
                act.activation(probT[:, g % 2, 0, 0:n, :], pt_ps[0][:, 0:n, :], ACT.Copy).then_inc(pt_ready[0], 1)

            def exponent(s, a):
                p, i = pair_of_step(s)
                n = P * key_tiles(s)
                act.wait_ge(biased[a], s + 1)
                act.activation(prob[:, a, s % 2, 0:n], prob[:, a, s % 2, 0:n], ACT.Exp, scale=-1.0,
                               bias=nmax[:, a, s % 2:s % 2 + 1],
                               accum_out=lsum[:, p % 2, i, a:a + 1]).then_inc(prob_ready[a], 1)

            for s in range(STEPS + 1):
                if s < STEPS and v_turn_of_step(s):
                    evacuate(m)
                    m += 1
                if s >= 1:
                    copy_probT(s - 1, 0)
                if s < STEPS:
                    exponent(s, 0)
                    exponent(s, 1)
                if s >= 1 and len(chunks(s - 1)) == 2:
                    copy_probT(s - 1, 1)
                if s < STEPS:
                    p, i = pair_of_step(s)
                    if projection_of_step(s):
                        while next_w < min(projection_of_step(s)[0] + 2, N_W):
                            split_hi(next_w)
                            next_w += 1
                        evacuate(m)
                        m += 1
                    if (p, i) >= (NP - 2, 4):
                        n = (p - NP + 2) * NT + i - 4
                        if n < NP:
                            act.wait_ge(wo_in, 16 * (n + 1))
                            act.wait_ge(j_done, projected(N_W - 1))
                            act.activation(wo_hi[:, n, :], w_raw[:, :, :].rearrange("p k m -> p (k m)"),
                                           ACT.Copy).then_inc(wo_hi_ready, 1)
            assert m == len(uses)

            def mixed_hi(t):
                cut = slice(P * t, P * t + P)
                act.wait_ge(og_ready, 2 * NP)
                if t >= 2:
                    act.wait_ge(out_done, t - 1)
                act.activation(w_hl[:, t % 2, 0, 0:6, :], og[:, :, cut], ACT.Copy)
                act.activation(w_hl[:, t % 2, 0, 6:8, :], k_sb[:, :, cut], ACT.Copy).then_inc(og_hi_ready, 1)

            act.wait_ge(j_done, projected(N_W - 1))
            mixed_hi(0)
            mixed_hi(1)
            act.wait_ge(gf_in, 16)
            for t in range(NT):
                act.wait_ge(y_ready, t + 1)
                if t >= 1:
                    act.wait_ge(ysq_ready, t)
                act.activation(sq_junk, y_row[t % 2], ACT.Square,
                               accum_out=stat[:, 0, t:t + 1]).then_inc(ysq_ready, 1)
                if t + 2 < NT:
                    mixed_hi(t + 2)
                act.wait_ge(yvar_ready, t + 1)
                act.activation(stat[:, 2, t:t + 1], stat[:, 1, t:t + 1], ACT.Sqrt).then_inc(yroot_ready, 1)

        @block.vector
        def _(dve):
            chain = [0]

            def link(ins):
                chain[0] += 1
                ins.then_inc(dve_seq, 1)
                dve.wait_ge(dve_seq, chain[0])

            def variance(a, b, ready):
                dve.tensor_scalar(stat[:, 1, a:b], stat[:, 0, a:b], 1.0 / D, EPS, ALU.mult, ALU.add).then_inc(ready, 1)

            def inverse_root(a, b):
                v, r, y, t = (stat[:, n, a:b] for n in range(1, 5))
                link(dve.reciprocal(y, r))
                link(dve.tensor_tensor(t, y, y, ALU.mult))
                link(dve.tensor_tensor(t, t, v, ALU.mult))
                link(dve.tensor_scalar(t, t, -0.5, 1.5, ALU.mult, ALU.add))
                link(dve.tensor_tensor(y, y, t, ALU.mult))

            scaled = [0]

            def scale_tile(r):
                if scaled[0] >= 2:
                    dve.wait_ge(turned, 2 * (scaled[0] - 1))
                dve.scalar_tensor_tensor(out=x_scaled[r % 2], in0=x_raw[r], scalar=stat[:, 3, r:r + 1],
                                         in1=(gm_row if r < MT else g_row), op0=ALU.mult,
                                         op1=ALU.mult).then_inc(x_ready, 1)
                scaled[0] += 1

            def low(u):
                r, b = u // 2, u % 2
                dve.wait_ge(hi_ready, u + 1)
                at = (slice(None), slice(4 * b, 4 * b + 4), slice(P * (r - MT), P * (r - MT) + P))
                dve.tensor_tensor(h_lo[at], turn_banks[u % 6].rearrange("p (k t) -> p k t", k=4),
                                  h_hi[at].bitcast(F32), ALU.subtract).then_inc(lo_ready, 1)

            batches = ((0, MT), (MT, MT + 4), (MT + 4, MT + NT))
            for n, (a, b) in enumerate(batches):
                dve.wait_ge(squares_ready, b)
                variance(a, b, var_ready)
                dve.wait_ge(root_ready, n + 1)
                inverse_root(a, b)
                if n == 0:
                    dve.wait_ge(rows_in, 32)
                if n < 2:
                    for r in range(a, a + 2):
                        scale_tile(r)
            for r in range(MT + 2, MT + NT):
                low(2 * (r - 2))
                low(2 * (r - 2) + 1)
                scale_tile(r)
            low(2 * (MT + NT - 2))
            low(2 * (MT + NT - 2) + 1)
            low(2 * (MT + NT - 1))
            low(2 * (MT + NT - 1) + 1)

            for u, (i, h) in enumerate(IDX_UNITS):
                if u == 0:
                    dve.wait_ge(j_free, use_number[("bturn", 0, 1)] + 1)
                dve.wait_ge(relu_ready, u + 1)
                n = P * (i + 1)
                wt = w_i[:, i, h:h + 1]
                if h == 0:
                    dve.tensor_scalar(x_slice(i), relu[u % 4][:, 0:n], wt, None, ALU.mult).then_inc(idx_added, 1)
                else:
                    dve.wait_ge(idx_added, u)
                    dve.scalar_tensor_tensor(out=x_slice(i), in0=relu[u % 4][:, 0:n], scalar=wt, in1=x_slice(i),
                                             op0=ALU.mult, op1=ALU.add).then_inc(idx_added, 1)
                if h == H_I - 1:
                    dve.wait_ge(idx_added, u + 1)
                    dve.tensor_reduce(reach[:, i - FIRST_TOPK:i - FIRST_TOPK + 1], x_slice(i), AX_X, ALU.max,
                                      apply_absolute_value=True).then_inc(reach_ready, 1)

            def choose(t, slot):
                xs, n = x_slice(t), P * (t + 1)
                level, step, count, extra, flag, late = (tk[:, c:c + 1] for c in (0, 1, 2, 3, 5, 4))
                some = picked[:, 0:n]
                if slot == 0:
                    if t > FIRST_TOPK:
                        dve.wait_ge(mask_ready, t - FIRST_TOPK)
                        dve.wait_ge(spoiled_any, t - FIRST_TOPK)
                    link(dve.tensor_copy(step, reach[:, t - FIRST_TOPK:t - FIRST_TOPK + 1]))
                    link(dve.memset(level, 0.0))
                elif slot <= HALVINGS:
                    link(dve.tensor_scalar(some, xs, level, None, ALU.is_ge, ALU.add, accum_out=count))
                    link(dve.tensor_scalar(step, step, 0.5, None, ALU.mult))
                    link(dve.tensor_scalar(count, count, float(TOPK), 0.5, ALU.is_ge, ALU.subtract))
                    link(dve.tensor_scalar(count, count, 2.0, None, ALU.mult))
                    link(dve.scalar_tensor_tensor(out=level, in0=step, scalar=count, in1=level,
                                                  op0=ALU.mult, op1=ALU.add))
                elif slot == HALVINGS + 1:
                    link(dve.scalar_tensor_tensor(out=level, in0=step, scalar=-1.01, in1=level,
                                                  op0=ALU.mult, op1=ALU.add))
                    link(dve.tensor_scalar(some, xs[:, ::-1], level, None, ALU.is_lt, ALU.add, accum_out=count))
                    link(dve.tensor_scalar(extra, count, -1.0, float(n - TOPK), ALU.mult, ALU.add))
                elif slot == HALVINGS + 2:
                    link(dve.scalar_tensor_tensor(out=some, in0=some, scalar=NEVER, in1=xs[:, ::-1],
                                                  op0=ALU.mult, op1=ALU.subtract))
                    link(dve.tensor_scalar(late, extra, 7.5, None, ALU.is_gt))
                    dve.scalar_tensor_tensor(out=flag, in0=extra, scalar=-0.5, in1=late,
                                             op0=ALU.is_lt, op1=ALU.add).then_inc(spoiled, 1)
                elif slot == HALVINGS + 3:
                    if t == FIRST_TOPK:
                        dve.wait_ge(eight_ready, 1)
                    link(dve.max(cut8[:, 0, :], some))
                    link(dve.scalar_tensor_tensor(out=cut8[:, 0, :], in0=eight[:, :], scalar=extra,
                                                  in1=cut8[:, 0, :], op0=ALU.is_lt, op1=ALU.mult))
                    link(dve.tensor_scalar(cut8[:, 1, :], eight[:, :], extra, NEVER, ALU.is_ge, ALU.mult))
                    link(dve.tensor_tensor(cut8[:, 2, :], cut8[:, 0, :], cut8[:, 1, :], ALU.add))
                elif slot == HALVINGS + 4:
                    link(dve.match_replace(out=some, in_to_replace=cut8[:, 2, :], in_values=some, imm_value=NEVER))

            def settle(t):
                xs, n = x_slice(t), P * (t + 1)
                dve.wait_ge(spoiled_any, t - FIRST_TOPK + 1)
                rows = dve.value_load(failed[0:1, 0:1], min_val=0, max_val=P)
                with dve.If(rows > 0):
                    with dve.Fori(0, ROUNDS):
                        dve.max(cut8[:, 0, :], xs)
                        dve.drain()
                        dve.match_replace(out=xs, in_to_replace=cut8[:, 0, :], in_values=xs, imm_value=NEVER)
                        dve.drain()
                    dve.tensor_scalar(picked[:, 0:n], xs[:, ::-1], -2e38, NEVER, ALU.is_ge, ALU.mult)
                dve.drain().then_inc(topk_done, 1)

            def choose_slots(p, slots):
                for slot in slots:
                    choose(IDX_TILES[p], slot)

            def add_bias(s, a):
                p, i = pair_of_step(s)
                g = PAIRS[p][0]
                n = P * key_tiles(s)
                dve.wait_ge(scored[a], s + 1)
                if s >= 2:
                    dve.wait_ge(pt_done[a], CHUNK0[s - 1])
                low_out = nmax[:, a, s % 2:s % 2 + 1]
                dst = prob[:, a, s % 2, 0:n]
                if g == "M":
                    dve.tensor_scalar(dst, s_ps[a][:, 0:n], 1.0, 3e38, ALU.mult, ALU.min,
                                      accum_out=low_out).then_inc(biased[a], 1)
                    return
                if g == "A":
                    if i == 0:
                        dve.wait_ge(bias_in, 32 * (p - 1))
                    table = bias[:, a, T - n:T]
                else:
                    dve.wait_ge(bias_ready[a], s - 6 * NT + 1)
                    table = bias[:, a, 0:n]
                dve.tensor_tensor_reduce(dst, s_ps[a][:, 0:n], table, 1.0, 3e38, ALU.add, ALU.min,
                                         low_out).then_inc(biased[a], 1)

            def copy_probT(s, c):
                g = CHUNK0[s] + c
                dve.wait_ge(pt_done[1], g + 1)
                if g >= 2:
                    dve.wait_ge(pv_done, g - 1)
                n = len(chunks(s)[c])
                dve.tensor_copy(probT[:, g % 2, 1, 0:n, :], pt_ps[1][:, 0:n, :]).then_inc(pt_ready[1], 1)

            groups = [0]

            def finish_group(p, g):
                for a in range(2):
                    dve.wait_ge(prob_ready[a], p * NT + 4 * g + 4)
                inverse = lsum[:, p % 2, 4 * g:4 * g + 4, :]
                link(dve.reciprocal(inverse, inverse))
                dve.tensor_copy(linv[:, :, :, :], inverse.unsqueeze(3).broadcast_to([P, 4, 2, DH])).then_inc(linv_ready, 1)
                groups[0] += 1
                dve.wait_ge(gate_ready, p + 1)
                dve.wait_ge(linv_turned, groups[0])
                cut = slice(HALF * g, HALF * g + HALF)
                dve.tensor_tensor(gate[:, p % 2, cut], pt_ps[0][:, :, :].rearrange("p a b -> p (a b)"),
                                  gate[:, p % 2, cut], ALU.mult).then_inc(linv_used, 1)
                dve.wait_ge(linv_used, groups[0])
                dve.wait_ge(pv_done, CHUNK0[p * NT + 4 * g + 4])
                dve.tensor_tensor(og_of(p)[:, cut], o_ps[:, :], gate[:, p % 2, cut], ALU.mult).then_inc(og_ready, 1)

            for s in range(STEPS + 1):
                p, i = pair_of_step(s)
                if s >= 1:
                    copy_probT(s - 1, 0)
                if s < STEPS:
                    if i == 0 and p < len(IDX_TILES):
                        dve.wait_ge(idx_masked, p + 1)
                    add_bias(s, 0)
                    add_bias(s, 1)
                    if i == 0 and 1 <= p <= len(IDX_TILES):
                        settle(IDX_TILES[p - 1])
                    if i >= 1 and p < len(IDX_TILES):
                        choose_slots(p, CHOICE_SLOTS[2 * i - 2])
                if s >= 1 and len(chunks(s - 1)) == 2:
                    copy_probT(s - 1, 1)
                if s < STEPS and i >= 1 and p < len(IDX_TILES):
                    choose_slots(p, CHOICE_SLOTS[2 * i - 1])
                if s >= 1 and (s - 1) % 4 == 3:
                    finish_group(*(pair_of_step(s - 1)[0], (s - 1) % NT // 4))

            def add_residual(t):
                dve.wait_ge(out_done, t + 1)
                dve.wait_ge(xr_in[t % 2], 16 * (t // 2 + 1))
                if t >= 2:
                    dve.wait_ge(stored[t % 2], 16 * (t // 2))
                dve.tensor_tensor(y_row[t % 2], s_ps[t % 2][:, :], x_res[t % 2], ALU.add).then_inc(y_ready, 1)
                dve.wait_ge(ysq_ready, t + 1)
                variance(t, t + 1, yvar_ready)

            def final_norm(t):
                dve.wait_ge(yroot_ready, t + 1)
                inverse_root(t, t + 1)
                dve.scalar_tensor_tensor(out=y_row[t % 2], in0=y_row[t % 2], scalar=stat[:, 3, t:t + 1], in1=gf_row,
                                         op0=ALU.mult, op1=ALU.mult).then_inc(y_final, 1)

            dve.wait_ge(gf_in, 16)
            for t in range(NT):
                add_residual(t)
                final_norm(t)

        @block.tensor
        def _(pe):
            pe.wait_ge(ident_ready, 2)

            def turn(u):
                r, b = u // 2, u % 2
                pe.wait_ge(x_ready, r + 1)
                if u >= 6:
                    pe.wait_ge(hi_ready, u - 5)
                if u - 6 >= 2 * MT:
                    pe.wait_ge(lo_ready, u - 5 - 2 * MT)
                for c in range(4):
                    k = 4 * b + c
                    last = pe.transpose(turn_banks[u % 6][:, P * c:P * c + P], x_scaled[r % 2][:, P * k:P * k + P],
                                        ident[:, :])
                last.then_inc(turned, 1)

            m = 0

            def fill(m):
                kind, w, b = uses[m]
                bank = bank_of(m)
                if free_before(m) > 0:
                    pe.wait_ge(j_free, free_before(m))
                if kind == "mem":
                    pe.wait_ge(wm_in[w % 2], 16 * (w // 2 + 1))
                    for k in range(KD):
                        last = pe.matmul(bank[:, 0:N_MEM], wm_raw[:, w % 2, k, :], memT[:, k, :],
                                         start=(k == 0), stop=(k == KD - 1))
                elif kind == "memturn":
                    pe.wait_ge(j_free, m)
                    for t in range(MT):
                        for f in range(2):
                            at = N_MEM * t + P * f
                            last = pe.transpose(bank[:, at:at + P], vmT[:, f, P * t:P * t + P], ident[:, :])
                elif kind == "bturn":
                    pe.wait_ge(j_free, m)
                    for c in range(4):
                        last = pe.transpose(bank[:, 72 * c:72 * c + 72], vT[0:72, P * c:P * c + P], ident[0:72, 0:72])
                elif kind == "vturn":
                    for c in range(4):
                        last = pe.transpose(bank[:, P * c:P * c + P], vT[:, P * c:P * c + P], ident[:, :])
                else:
                    pe.wait_ge(w_lo_ready, w + 1)
                    n = width(w)
                    hi, lo = w_hl[:, w % 2, 0], w_hl[:, w % 2, 1]
                    passes = [(hi, h_hi), (hi, h_lo), (lo, h_hi)]
                    for k in range(KD):
                        for q, (a, c) in enumerate(passes):
                            last = pe.matmul(bank[0:n, :], a[:, k, 0:n], c[:, k, HALF * b:HALF * b + HALF],
                                             start=(k == 0 and q == 0), stop=(k == KD - 1 and q == 2))
                last.then_inc(j_done, 1)

            for u in range(2 * MT):
                turn(u)
            pe.wait_ge(hi_ready, 2 * MT)
            for _ in range(5):
                fill(m)
                m += 1
            for u in range(2 * MT, 2 * (MT + NT)):
                turn(u)
            pe.wait_ge(lo_ready, 2 * NT)
            while uses[m] != ("w", *PRE_PAIR_HALVES[0]):
                fill(m)
                m += 1
            for u, (i, h) in enumerate(IDX_UNITS):
                if h == 0 and i - FIRST_TOPK < len(PRE_PAIR_HALVES):
                    fill(m)
                    m += 1
                if u == 0:
                    pe.wait_ge(j_free, use_number[("w", FIRST_W[0] - 1, 1)] + 1)
                if u >= 2:
                    pe.wait_ge(relu_ready, u - 1)
                r = slice(DH * (h % 2), DH * (h % 2) + DH)
                for c in range(0, P * (i + 1), HALF):
                    n = min(HALF, P * (i + 1) - c)
                    last = pe.matmul(s_ps[u % 2][:, c:c + n], q_i[r, h // 2, P * i:P * i + P], k_i[r, c:c + n],
                                     start=True, stop=True)
                last.then_inc(idx_scored, 1)

            def scores(s, a):
                p, i = pair_of_step(s)
                g = PAIRS[p][0]
                if i == 0 and a == 0:
                    pe.wait_ge(j_free, evacuated(p, "q"))
                    if g == "A":
                        pe.wait_ge(j_free, use_number[("vturn", p, 1)] + 1)
                if s == 0:
                    pe.wait_ge(relu_ready, len(IDX_UNITS))
                else:
                    pe.wait_ge(biased[a], s)
                r = slice(DH * a, DH * a + DH)
                keys = {"A": k_sb[:, p % 2, :], "B": k_b[:, :], "M": k_m[:, PAIRS[p][1], :] if g == "M" else None}[g]
                n_keys = P * key_tiles(s)
                for c in range(0, n_keys, HALF):
                    n = min(HALF, n_keys - c)
                    last = pe.matmul(s_ps[a][:, c:c + n], q_sb[r, p % 2, P * i:P * i + P], keys[r, c:c + n],
                                     start=True, stop=True)
                last.then_inc(scored[a], 1)

            def turn_prob(s, c):
                g = CHUNK0[s] + c
                for a in range(2):
                    pe.wait_ge(prob_ready[a], s + 1)
                    if g >= 1:
                        pe.wait_ge(pt_ready[a], g)
                    if a == 0 and s // 4 >= 1:
                        pe.wait_ge(linv_used, s // 4)
                    for n, k in enumerate(chunks(s)[c]):
                        last = pe.transpose(pt_ps[a][:, n, :], prob[:, a, s % 2, P * k:P * k + P], ident[:, :])
                    last.then_inc(pt_done[a], 1)

            def values(s, c):
                p, i = pair_of_step(s)
                g = CHUNK0[s] + c
                pr, j = PAIRS[p][0], PAIRS[p][1]
                for a in range(2):
                    pe.wait_ge(pt_ready[a], g + 1)
                if i % 4 == 0 and c == 0 and s >= 4:
                    pe.wait_ge(og_ready, s // 4)
                at = slice(P * (i % 4), P * (i % 4) + P)
                nk = key_tiles(s)
                for n, k in enumerate(chunks(s)[c]):
                    for a in range(2):
                        if pr == "A":
                            v = v_sb[:, p % 2, k, DH * a:DH * a + DH]
                        elif pr == "B":
                            v = v_b[:, k, :]
                        else:
                            v = v_m[:, k, P * j + DH * a:P * j + DH * a + DH]
                        last = pe.matmul(o_ps[DH * a:DH * a + DH, at], v, probT[:, g % 2, a, n, :],
                                         start=(k == 0), stop=(k == nk - 1))
                last.then_inc(pv_done, 1)

            def turn_sums(s):
                p, i = pair_of_step(s)
                pe.wait_ge(linv_ready, s // 4 + 1)
                pe.wait_ge(pt_ready[0], CHUNK0[s + 1])
                for c in range(4):
                    last = pe.transpose(pt_ps[0][:, c, :], linv[:, c, :, :].rearrange("p a f -> p (a f)"), ident[:, :])
                last.then_inc(linv_turned, 1)

            for s in range(STEPS + 1):
                if s < STEPS and v_turn_of_step(s):
                    fill(m)
                    m += 1
                if s >= 1:
                    turn_prob(s - 1, 0)
                if s < STEPS:
                    scores(s, 0)
                    scores(s, 1)
                if s >= 1:
                    values(s - 1, 0)
                    if len(chunks(s - 1)) == 2:
                        turn_prob(s - 1, 1)
                if s < STEPS and projection_of_step(s):
                    fill(m)
                    m += 1
                if s >= 1:
                    if len(chunks(s - 1)) == 2:
                        values(s - 1, 1)
                    if (s - 1) % 4 == 3:
                        turn_sums(s - 1)
            assert m == len(uses)

            pe.wait_ge(wo_lo_ready, NP)
            for t in range(NT):
                pe.wait_ge(og_lo_ready, t + 1)
                if t >= 2:
                    pe.wait_ge(y_ready, t - 1)
                hi, lo = w_hl[:, t % 2, 0], w_hl[:, t % 2, 1]
                passes = [(hi, wo_hi), (hi, wo_lo), (lo, wo_hi)]
                for b in range(2):
                    cut = slice(HALF * b, HALF * b + HALF)
                    for p in range(NP):
                        for q, (a, c) in enumerate(passes):
                            last = pe.matmul(s_ps[t % 2][:, cut], a[:, p, :], c[:, p, cut],
                                             start=(p == 0 and q == 0), stop=(p == NP - 1 and q == 2))
                last.then_inc(out_done, 1)


def distance_table():
    d = np.arange(P)[:, None] + (T - P) - np.arange(T)[None, :]
    return d, np.where(d >= 0, d, BIG).astype(np.float32)


def window_tables():
    d, _ = distance_table()
    count = np.zeros(d.shape)
    for window, dilation in ((128, 1), (512, 4), (2048, 16)):
        count += (d >= 0) & (d % dilation == 0) & (d <= window)
    heads = []
    for h in range(H_A):
        slope = 2.0 ** (-8.0 * (h + 1) / H_A)
        heads.append(np.where(count > 0, slope * d - np.log(np.maximum(count, 1)), BIG))
    return np.stack(heads).astype(np.float32)


_INS = ["x", "mem", "g_in", "g_mem", "w_in", "w_mem_kv", "w_out", "g_final"]


def kernel(**inputs):
    import numpy as _np
    import concourse.bacc as _bacc
    from concourse import mybir as _mybir
    from concourse.bass_utils import run_bass_kernel_spmd as _run

    nc = _bacc.Bacc("TRN2", target_bir_lowering=False, num_devices=1)
    arrays, args = {}, []
    tables = {"dist_tab": distance_table()[1], "a_tab": window_tables()}
    for name in _INS + list(tables):
        a = _np.ascontiguousarray(tables[name] if name in tables else inputs[name])
        arrays[f"in_{name}_dram"] = a
        args.append(nc.dram_tensor(f"in_{name}_dram", a.shape, _mybir.dt.from_np(a.dtype), kind="ExternalInput").ap())
    args.append(nc.dram_tensor("out_0_dram", (1, T, D), F32, kind="ExternalOutput").ap())
    build_program(nc, *args)
    r = _run(nc, [arrays], core_ids=[0])
    return r.results[0]["out_0_dram"]
```

```python
import math
from contextlib import ExitStack

import numpy as np

import concourse.bass as bass
from concourse import mybir

F32 = mybir.dt.float32
F32R = mybir.dt.float32r
ALU = mybir.AluOpType
ACT = mybir.ActivationFunctionType
AX_X = mybir.AxisListType.X

P = 128
T = 1024
D = 1024
KD = D // P
NT = T // P
N_MEM = 256
MT = N_MEM // P
DH = 64
HALF = 512
H_A, H_B, H_M, H_I = 8, 4, 4, 8
TOPK = 256
FIRST_TOPK = TOPK // P
EPS = 1e-6
BIG = 1e30

C_QA, C_KA, C_VA = 0, 512, 1024
C_QB = 1536
C_KB = C_QB + H_B * DH
C_VB = C_KB + DH
C_QM = C_VB + DH
C_GATE = C_QM + H_M * DH
C_QI = C_GATE + 1024
C_KI = C_QI + H_I * DH
C_WI = C_KI + DH

PAIRS = [("M", 0, 6), ("M", 1, 7), ("A", 0, 0), ("A", 1, 1), ("A", 2, 2), ("A", 3, 3), ("B", 0, 4), ("B", 1, 5)]
NP = len(PAIRS)
STEPS = NP * NT


GATES_WITH = {NP - 2: [NP - 2, NP - 1], NP - 1: []}


def w_tiles():
    def q_tile(p):
        g, j, _ = PAIRS[p]
        return "q", p, [({"A": C_QA, "B": C_QB, "M": C_QM}[g] + P * j, P)]

    out = [("kIwI", None, [(C_KI, DH), (C_WI, H_I)])]
    out += [("qI", j, [(C_QI + P * j, P)]) for j in range(H_I // 2)]
    out += [q_tile(0)]
    for p, (g, j, f) in enumerate(PAIRS):
        follows = PAIRS[p + 1][:2] if p + 1 < NP else None
        if follows and follows[0] == "A":
            out += [("k", p + 1, [(C_KA + P * follows[1], P)])]
        if follows == ("B", 0):
            out += [("kvB", p + 1, [(C_KB, DH), (C_VB, DH)])]
        out += [("gate", q, [(C_GATE + P * PAIRS[q][2], P)]) for q in GATES_WITH.get(p, [p])]
        if follows and follows[0] == "A":
            out += [("v", p + 1, [(C_VA + P * follows[1], P)])]
        if follows:
            out += [q_tile(p + 1)]
    return out


W_TILES = w_tiles()
W_OF = {(what, p): n for n, (what, p, _) in enumerate(W_TILES)}
N_W = len(W_TILES)
PRE_W = W_OF["gate", 0] + 1
SLOT = {"k": 0, "kvB": 0, "gate": 2, "v": 4, "q": 6}


def slope_of(p, a):
    return 2.0 ** (-8.0 * (2 * PAIRS[p][1] + a + 1) / H_B)


def query_scale(p, a):
    return -(DH ** -0.5) / (slope_of(p, a) if PAIRS[p][0] == "B" else 1.0)


def width(w):
    return sum(n for _, n in W_TILES[w][2])


def pair_of_step(s):
    return s // NT, s % NT


def key_tiles(s):
    p, i = pair_of_step(s)
    return MT if PAIRS[p][0] == "M" else i + 1


def chunks(s):
    n = key_tiles(s)
    return [range(c, min(c + 4, n)) for c in range(0, n, 4)]


CHUNK0 = [sum(len(chunks(q)) for q in range(s)) for s in range(STEPS + 1)]


def projection_of_step(s):
    p, i = pair_of_step(s)
    for what, at in SLOT.items():
        w = W_OF.get((what, p if what == "gate" else p + 1))
        if (what, p) == ("v", NP - 2):
            w = W_OF["gate", NP - 1]
        if w is not None and w >= PRE_W and i in (at, at + 1) and (what, p) != ("gate", NP - 1):
            return w, i - at
    return None


def coming(s):
    for q in range(s, STEPS):
        if projection_of_step(q):
            return projection_of_step(q)[0]
    return N_W


WO_PER_STEP = 2
WO_ROOMS = 3
EARLY = NT // 2
EARLY_OUT = {STEPS - 3: (None, (0, 0), None), STEPS - 2: ((0, 1), (1, 0), None),
             STEPS - 1: ((1, 1), (2, 0), None), STEPS: ((2, 1), (3, 0), (3, 1))}


def wo_of_step(s):
    n = (s - (STEPS - NT)) * WO_PER_STEP
    return range(max(n, 0), max(min(n + WO_PER_STEP, NP), 0))


def v_turn_of_step(s):
    if s == 0 or projection_of_step(s - 1) is None:
        return None
    w, b = projection_of_step(s - 1)
    return (W_TILES[w][1], b) if W_TILES[w][0] in ("v", "kvB") else None


IDX_TILES = list(range(FIRST_TOPK, NT))
IDX_UNITS = [(i, h) for i in IDX_TILES for h in range(H_I)]
X_OFF = {i: sum(P * (q + 1) for q in range(FIRST_TOPK, i)) for i in IDX_TILES}
X_COLS = sum(P * (q + 1) for q in IDX_TILES)
PRE_PAIR_HALVES = [(W_OF[what, 0], b) for what in ("q", "gate") for b in range(2)]
K_SLOT = [2, 5]
ROUNDS = TOPK // 8
HALVINGS = 12
NEVER = -3e38
CHOICE_SLOTS = [[q for q in range(HALVINGS + 5) if q * 2 * (NT - 1) // (HALVINGS + 5) == n] for n in range(2 * (NT - 1))]


def build_program(nc, x, mem, g_in, g_mem, w_in, w_mem, w_out, g_final, dist_tab, a_tab, out):
    with ExitStack() as ctx:
        def sb(name, shape, dt=F32):
            return ctx.enter_context(nc.sbuf_tensor(name, shape, dt))

        def sem(name):
            return ctx.enter_context(nc.semaphore(name))

        h_hi = sb("h_hi", [P, KD, T], F32R)
        h_lo = sb("h_lo", [P, KD, T], F32R)
        w_hl = sb("w_hl", [P, 2, 2, KD, P], F32R)
        w_raw = sb("w_raw", [P, KD, P])
        qk = sb("qk", [P, 8, T], F32R)
        kk_b = sb("kk_b", [P, 2, T], F32R)
        v_sb = sb("v_sb", [P, 2, NT, P])
        vT = sb("vT", [P, HALF])
        gate = sb("gate", [P, T])
        v_b = sb("v_b", [P, NT, DH])
        w_i = sb("w_i", [P, NT, H_I])
        bias = sb("bias", [P, 2, T])
        prob = sb("prob", [P, 2, 2, T])
        probT = sb("probT", [P, 2, 2, 4, P])
        idx = sb("idx", [P, X_COLS])
        mixed_dram = nc.dram_tensor("mixed_scratch", (NP - 1, P, T), F32, kind="Internal").ap()
        dist = sb("dist", [P, T])
        ident = sb("ident", [P, P])
        lsum = sb("lsum", [P, 2, NT, 2])
        linv = sb("linv", [P, 4, 2, DH])
        nmax = sb("nmax", [P, 2, 2])
        picked = sb("picked", [P, T])
        cut8 = sb("cut8", [P, 3, 8])
        eight = sb("eight", [P, 8])
        tk = sb("tk", [P, 8])
        reach = sb("reach", [P, len(IDX_TILES)])
        failed = sb("failed", [P, 1], mybir.dt.int32)
        stat = sb("stat", [P, 5, MT + NT])
        q_i = qk[:, :, :]
        kk_i = kk_b[:, :, :]
        x_rooms = [idx[:, 0:T], idx[:, T:2 * T], idx[:, 2 * T:3 * T], picked[:, :], idx[:, 3 * T:4 * T],
                   dist[:, :], bias[:, 1, :]]
        V_M_ROOM = 3
        x_raw = [x_rooms[r % len(x_rooms)] for r in range(MT + NT)]
        x_scaled = [prob[:, 0, 0, :], prob[:, 0, 1, :]]
        g_row, gm_row = prob[:, 1, 0, :], prob[:, 1, 1, :]
        q_m = v_sb[:, 1, :, :].rearrange("p t f -> p (t f)")
        memT = v_sb[:, :, :, :].rearrange("p a b c -> p (a b c)").rearrange("p (k m) -> p k m", k=KD)
        wm_raw = probT[:, :, :, :, :].rearrange("p a b c d -> p (a b c d)").rearrange("p (a k m) -> p a k m", a=2, k=KD)
        relu = [prob[:, 0, 0, :], prob[:, 0, 1, :], prob[:, 1, 0, :], prob[:, 1, 1, :]]
        k_m = bias[:, 0, 0:2 * N_MEM].rearrange("p (a m) -> p a m", a=2)
        v_m = picked[:, T - 2 * N_MEM:T].rearrange("p (t f) -> p t f", t=MT)
        vmT = vT[:, 0:2 * N_MEM].rearrange("p (a m) -> p a m", a=2)
        wo_hi, wo_lo = h_hi, h_lo
        wo_raw = [bias[:, 0, :], bias[:, 1, :], w_raw[:, :, :].rearrange("p k m -> p (k m)")]
        y_rows = [gate[:, :], v_sb[:, 1, :, :].rearrange("p t f -> p (t f)"), dist[:, :], picked[:, :],
                  prob[:, 0, 0, :], prob[:, 1, 0, :], prob[:, 0, 1, :], prob[:, 1, 1, :]]
        gf_row = idx[:, 0:T]
        sq_junk = qk[:, 2, :]
        mixed = [bias[:, b, 0:(NP - 1) * P].rearrange("p (q t) -> p q t", q=NP - 1) for b in range(2)]

        s_ps = [ctx.enter_context(nc.psum_tensor(f"s_ps{a}", [P, T], F32)) for a in range(2)]
        pt_ps = [ctx.enter_context(nc.psum_tensor(f"pt_ps{a}", [P, 4, P], F32)) for a in range(2)]
        o_ps = ctx.enter_context(nc.psum_tensor("o_ps", [P, HALF], F32))
        j_ps = ctx.enter_context(nc.psum_tensor("j_ps", [P, HALF], F32))
        j_banks = [j_ps, o_ps]
        turn_banks = [s_ps[0][:, 0:HALF], s_ps[0][:, HALF:T], s_ps[1][:, 0:HALF], s_ps[1][:, HALF:T],
                      pt_ps[0][:, :, :].rearrange("p a b -> p (a b)"), pt_ps[1][:, :, :].rearrange("p a b -> p (a b)")]

        x_in = [sem(f"x_in{r}") for r in range(MT + NT)]
        rows_in = sem("rows_in")
        consts_in = sem("consts_in")
        ident_ready = sem("ident_ready")
        eight_ready = sem("eight_ready")
        squares_ready = sem("squares_ready")
        var_ready = sem("var_ready")
        root_ready = sem("root_ready")
        x_ready = sem("x_ready")
        turned = sem("turned")
        hi_ready = sem("hi_ready")
        lo_ready = sem("lo_ready")
        wm_in = [sem("wm_in0"), sem("wm_in1")]
        w_in_sem = sem("w_in_sem")
        w_hi_ready = sem("w_hi_ready")
        w_lo_ready = sem("w_lo_ready")
        j_done = sem("j_done")
        j_free = sem("j_free")
        j_split = sem("j_split")
        gate_ready = sem("gate_ready")
        idx_scored = sem("idx_scored")
        relu_ready = sem("relu_ready")
        idx_added = sem("idx_added")
        reach_ready = sem("reach_ready")
        idx_masked = sem("idx_masked")
        spoiled = sem("spoiled")
        spoiled_any = sem("spoiled_any")
        topk_done = sem("topk_done")
        half_mask = sem("half_mask")
        mask_ready = sem("mask_ready")
        bias_in = sem("bias_in")
        scored = [sem("scored_a"), sem("scored_b")]
        biased = [sem("biased_a"), sem("biased_b")]
        prob_ready = [sem("prob_ready_a"), sem("prob_ready_b")]
        pt_done = [sem("pt_done_a"), sem("pt_done_b")]
        pt_ready = [sem("pt_ready_a"), sem("pt_ready_b")]
        pv_done = sem("pv_done")
        linv_ready = sem("linv_ready")
        linv_turned = sem("linv_turned")
        linv_used = sem("linv_used")
        og_ready = sem("og_ready")
        og_stored = [sem("og_stored0"), sem("og_stored1")]
        mixed_in = [sem("mixed_in0"), sem("mixed_in1")]
        wo_in = [sem(f"wo_in{n}") for n in range(WO_ROOMS)]
        wo_hi_ready = sem("wo_hi_ready")
        wo_lo_ready = sem("wo_lo_ready")
        gf_in = sem("gf_in")
        xr_in = [sem(f"xr_in{t}") for t in range(NT)]
        mix_hi_ready = sem("mix_hi_ready")
        mix_lo_ready = sem("mix_lo_ready")
        last_hi_ready = sem("last_hi_ready")
        last_lo_ready = sem("last_lo_ready")
        out_done = sem("out_done")
        y_added = sem("y_added")
        ysq_ready = sem("ysq_ready")
        yvar_ready = sem("yvar_ready")
        yroot_ready = sem("yroot_ready")
        y_final = sem("y_final")
        stored = sem("stored")
        dve_seq = sem("dve_seq")

        x_t = x.rearrange("b (t p) d -> (b t) p d", p=P)
        mem_t = mem.rearrange("b (t p) d -> (b t) p d", p=P)
        w_k = w_in.rearrange("l (k p) c -> (l p) k c", p=P)
        wm_k = w_mem.rearrange("l (k p) c -> (l p) k c", p=P)
        wo_k = w_out.rearrange("l (f p) c -> (l f) p c", p=P)
        out_t = out.rearrange("b (t p) d -> (b t) p d", p=P)

        def gates(p):
            return gate[:, :] if p < NP - 1 else v_sb[:, 0, :, :].rearrange("p t f -> p (t f)")

        def dist_slice(i):
            return dist[:, T - P * (i + 1):T]

        def x_slice(i):
            return idx[:, X_OFF[i]:X_OFF[i] + P * (i + 1)]

        def dist_of(i):
            return dist_slice(i) if i < FIRST_TOPK else x_slice(i)

        uses = [("mem", w, 0) for w in range(4)] + [("memturn", 0, 0)]
        uses += [(kind, 0, b) for b in range(2) for kind in ("w", "wturn")]
        uses += [("w", w, b) for w in range(1, W_OF["q", 0]) for b in range(2)]
        uses += [("w", w, b) for w, b in PRE_PAIR_HALVES]
        n_pre = len(uses)
        for s in range(STEPS):
            if v_turn_of_step(s):
                uses.append(("vturn", *v_turn_of_step(s)))
            if projection_of_step(s):
                uses.append(("w", *projection_of_step(s)))
        use_number = {u: m for m, u in enumerate(uses)}

        def bank_of(m):
            return j_banks[m % 2] if m < n_pre else j_ps

        def is_split(m):
            kind, w, _ = uses[m]
            what, p, _ = W_TILES[w] if kind == "w" else (None, None, None)
            return what in ("kIwI", "qI", "k", "kvB") or (what == "q" and PAIRS[p][0] != "M")

        def splits(m):
            return sum(is_split(q) for q in range(m))

        def free_before(m):
            return m - 1 if m < n_pre else m

        def wait_evacuated(eng, m):
            eng.wait_ge(j_free, m + 1)
            if splits(m + 1):
                eng.wait_ge(j_split, splits(m + 1))

        def projected(w):
            return use_number[("w", w, 1)] + 1

        block = ctx.enter_context(nc.Block())

        @block.sync
        def _(sp):
            sp.dma_start(x_raw[0], mem_t[0]).then_inc(x_in[0], 16)
            sp.dma_start(x_raw[1], mem_t[1]).then_inc(x_in[1], 16)
            sp.dma_start(gm_row, g_mem.broadcast_to([P, D])).then_inc(rows_in, 16)
            sp.dma_start(wm_raw[:, 0], wm_k[:, :, 0:P]).then_inc(wm_in[0], 16)
            for t in range(4):
                sp.dma_start(x_raw[MT + t], x_t[t]).then_inc(x_in[MT + t], 16)
            sp.dma_start(g_row, g_in.broadcast_to([P, D])).then_inc(rows_in, 16)

            def load_w(w):
                if w:
                    sp.wait_ge(w_hi_ready, w)
                    sp.wait_ge(w_lo_ready, w)
                at = 0
                for c, n in W_TILES[w][2]:
                    sp.dma_start(w_raw[:, :, at:at + n], w_k[:, :, c:c + n]).then_inc(w_in_sem, 16)
                    at += n

            load_w(0)
            sp.dma_start(wm_raw[:, 1], wm_k[:, :, P:2 * P]).then_inc(wm_in[1], 16)
            for t in range(4, NT):
                r = MT + t
                if r >= len(x_rooms):
                    sp.wait_ge(x_ready, r - len(x_rooms) + 1)
                sp.dma_start(x_raw[r], x_t[t]).then_inc(x_in[r], 16)
            load_w(1)
            for w in range(2, 4):
                sp.wait_ge(j_done, w - 1)
                sp.dma_start(wm_raw[:, w % 2], wm_k[:, :, P * w:P * w + P]).then_inc(wm_in[w % 2], 16)
            sp.wait_ge(x_ready, len(x_rooms) - 1)
            sp.dma_start(dist[:, :], dist_tab).then_inc(consts_in, 16)
            next_w = 2

            def load_ahead(w):
                nonlocal next_w
                while next_w < min(w, N_W):
                    load_w(next_w)
                    next_w += 1

            def store_mixed(p, g):
                cut = slice(HALF * g, HALF * g + HALF)
                sp.wait_ge(og_ready, 2 * p + g + 1)
                sp.dma_start(mixed_dram[p][:, cut], gates(p)[:, cut]).then_inc(og_stored[g], 16)

            def load_wo(n):
                if n == WO_ROOMS - 1:
                    sp.wait_ge(w_hi_ready, N_W)
                    sp.wait_ge(w_lo_ready, N_W)
                if n >= WO_ROOMS:
                    sp.wait_ge(wo_hi_ready, n - WO_ROOMS + 1)
                    sp.wait_ge(wo_lo_ready, n - WO_ROOMS + 1)
                sp.dma_start(wo_raw[n % WO_ROOMS], wo_k[PAIRS[n][2]]).then_inc(wo_in[n % WO_ROOMS], 16)

            def load_residual(t):
                sp.dma_start(y_rows[t], x_t[t]).then_inc(xr_in[t], 16)

            def load_mixed(t):
                sp.wait_ge(og_stored[t // EARLY], 16 * (NP - 1))
                if t >= 2:
                    sp.wait_ge(mix_hi_ready, t - 1)
                    sp.wait_ge(mix_lo_ready, t - 1)
                sp.dma_start(mixed[t % 2], mixed_dram[:, :, P * t:P * t + P].rearrange("q p t -> p q t")) \
                    .then_inc(mixed_in[t % 2], 16)

            load_ahead(PRE_W + 1)
            for s in range(STEPS):
                p, i = pair_of_step(s)
                if i == 0 and PAIRS[p][0] == "A":
                    for a in range(2):
                        sp.wait_ge(biased[a], s)
                        if PAIRS[p - 1][0] == "M":
                            sp.wait_ge(biased[1 - a], s)
                        sp.dma_start(bias[:, a, :], a_tab[2 * PAIRS[p][1] + a]).then_inc(bias_in, 16)
                if s >= 1 and i % 4 == 0 and s <= (NP - 1) * NT:
                    store_mixed((s - 1) // NT, (s - 1) % NT // 4)
                load_ahead(coming(s) + 3)
                last = s - (STEPS - NT)
                if last == -NT:
                    load_wo(0)
                    load_wo(1)
                if last >= 0:
                    for n in wo_of_step(s):
                        if n + WO_ROOMS - 1 < NP:
                            load_wo(n + WO_ROOMS - 1)
                if last == 2:
                    for g in range(2):
                        sp.wait_ge(og_stored[g], 16 * (NP - 1))
                    load_residual(0)
                    sp.wait_ge(pv_done, CHUNK0[STEPS - 2 * NT])
                    load_residual(1)
                    for a in range(2):
                        sp.wait_ge(biased[a], s)
                    load_residual(2)
                    sp.wait_ge(mask_ready, len(IDX_TILES))
                    load_residual(3)
                if last == 4:
                    for b in range(2):
                        sp.wait_ge(wo_lo_ready, NP - 1 + b)
                        load_mixed(b)
                if last == 5:
                    for a in range(2):
                        sp.wait_ge(biased[a], s)
                    sp.dma_start(gf_row, g_final.unsqueeze(0).broadcast_to([P, D])).then_inc(gf_in, 16)
                if last == 6:
                    load_mixed(2)
            assert next_w == N_W
            for parity in range(2):
                for a in range(2):
                    sp.wait_ge(pt_done[a], CHUNK0[STEPS - 1 + parity])
                    load_residual(EARLY + 2 * parity + a)
                load_mixed(3 + parity)
            load_mixed(5)
            load_mixed(6)
            for t in range(NT):
                if t == EARLY:
                    load_mixed(7)
                sp.wait_ge(y_final, t + 1)
                sp.dma_start(out_t[t], y_rows[t]).then_inc(stored, 16)
            sp.wait_ge(stored, 16 * NT)

        @block.gpsimd
        def _(pool):
            pool.memset(ident[:, :], 0.0).then_inc(ident_ready, 1)
            pool.wait_ge(ident_ready, 1)
            pool.affine_select(out=ident[:, :], in_=ident[:, :], compare_op=ALU.not_equal, fill=1.0, base=0,
                               pattern=[[-1, P]], channel_multiplier=1).then_inc(ident_ready, 1)

            def split_lo(w):
                pool.wait_ge(w_hi_ready, w + 1)
                n = width(w)
                pool.tensor_tensor(w_hl[:, w % 2, 1, :, 0:n], w_raw[:, :, 0:n],
                                   w_hl[:, w % 2, 0, :, 0:n].bitcast(F32), ALU.subtract).then_inc(w_lo_ready, 1)

            pool.iota(eight[:, :], pattern=[[1, 8]], base=0, channel_multiplier=0,
                      allow_small_or_imprecise_dtypes=True).then_inc(eight_ready, 1)
            for w in range(PRE_W):
                split_lo(w)
            for n, i in enumerate(IDX_TILES):
                pool.wait_ge(reach_ready, n + 1)
                diagonal = x_slice(i)[:, P * i:P * (i + 1)]
                pool.affine_select(out=diagonal, in_=diagonal, compare_op=ALU.is_ge, fill=-BIG, base=0,
                                   pattern=[[-1, P]], channel_multiplier=1).then_inc(idx_masked, 1)
            pool.wait_ge(consts_in, 16)
            next_w = PRE_W
            masks = 0
            for s in range(STEPS):
                p, i = pair_of_step(s)
                if i == 0 and 1 <= p <= len(IDX_TILES):
                    pool.wait_ge(spoiled, p)
                    pool.partition_all_reduce(failed[:, :], tk[:, 5:6], P, bass.bass_isa.ReduceOp.add)\
                        .then_inc(spoiled_any, 1)
                if i == 1 and 1 <= p <= len(IDX_TILES):
                    t = IDX_TILES[p - 1]
                    n = P * (t + 1)
                    pool.wait_ge(topk_done, p)
                    pool.tensor_scalar(x_slice(t), picked[:, n - 1::-1], -2e38, BIG,
                                       ALU.is_le, ALU.mult).then_inc(half_mask, 1)
                    masks += 1
                    pool.wait_ge(half_mask, masks)
                    pool.tensor_tensor(x_slice(t), x_slice(t), dist_slice(t), ALU.add).then_inc(mask_ready, 1)
                while next_w < min(coming(s) + 2, N_W):
                    split_lo(next_w)
                    next_w += 1
                for n in wo_of_step(s):
                    pool.wait_ge(wo_hi_ready, n + 1)
                    pool.tensor_tensor(wo_lo[:, n, :], wo_raw[n % WO_ROOMS],
                                       wo_hi[:, n, :].bitcast(F32), ALU.subtract).then_inc(wo_lo_ready, 1)
            def mix_lo(t):
                pool.wait_ge(mix_hi_ready, t + 1)
                pool.tensor_tensor(w_hl[:, t % 2, 1, 0:NP - 1, :], mixed[t % 2],
                                   w_hl[:, t % 2, 0, 0:NP - 1, :].bitcast(F32), ALU.subtract).then_inc(mix_lo_ready, 1)

            def last_lo(t):
                pool.wait_ge(last_hi_ready, t + 1)
                pool.tensor_tensor(w_hl[:, t % 2, 1, NP - 1, :], gates(NP - 1)[:, P * t:P * t + P],
                                   w_hl[:, t % 2, 0, NP - 1, :].bitcast(F32), ALU.subtract).then_inc(last_lo_ready, 1)

            mix_lo(0)
            mix_lo(1)
            last_lo(0)
            last_lo(1)
            for t in range(2, NT):
                mix_lo(t)
                last_lo(t)

        @block.scalar
        def _(act):

            def square_sums(rs):
                for r in rs:
                    act.wait_ge(x_in[r], 16)
                    if r >= 1:
                        act.wait_ge(squares_ready, r)
                    act.activation(gate[:, :], x_raw[r], ACT.Square,
                                   accum_out=stat[:, 0, r:r + 1]).then_inc(squares_ready, 1)

            def root(n, a, b):
                act.wait_ge(var_ready, n + 1)
                act.activation(stat[:, 2, a:b], stat[:, 1, a:b], ACT.Sqrt).then_inc(root_ready, 1)

            def split_hi(w):
                act.wait_ge(w_in_sem, 16 * sum(len(W_TILES[q][2]) for q in range(w + 1)))
                if w >= 2:
                    act.wait_ge(j_done, projected(w - 2))
                n = width(w)
                act.activation(w_hl[:, w % 2, 0, :, 0:n], w_raw[:, :, 0:n], ACT.Copy).then_inc(w_hi_ready, 1)

            def evacuate(m):
                kind, w, b = uses[m]
                bank = bank_of(m)
                act.wait_ge(j_done, m + 1)
                cut = slice(HALF * b, HALF * b + HALF)
                if kind == "mem":
                    dst = k_m[:, w, :] if w < 2 else vmT[:, w - 2, :]
                    last = act.activation(dst, bank[:, 0:N_MEM], ACT.Copy)
                elif kind == "memturn":
                    act.wait_ge(x_ready, V_M_ROOM + 1)
                    last = act.activation(v_m, bank[:, :].rearrange("p (t f) -> p t f", t=MT), ACT.Copy)
                elif kind == "wturn":
                    last = act.activation(w_i[:, 4 * b:4 * b + 4, :],
                                          bank[:, 0:4 * H_I].rearrange("p (t c) -> p t c", t=4), ACT.Copy,
                                          scale=float(H_I) ** -0.5)
                elif kind == "vturn":
                    if PAIRS[w][0] == "A":
                        last = act.activation(v_sb[:, w % 2, 4 * b:4 * b + 4, :].rearrange("p t f -> p (t f)"),
                                              bank[:, :], ACT.Copy)
                    else:
                        last = act.activation(v_b[:, 4 * b:4 * b + 4, :].rearrange("p t f -> p (t f)"),
                                              bank[:, 0:4 * DH], ACT.Copy)
                else:
                    what, p, _ = W_TILES[w]
                    if what in ("kIwI", "kvB"):
                        act.activation(kk_b[0:DH, 0, cut], bank[0:DH, :], ACT.Copy)
                        act.activation(kk_b[DH:P, 0, cut], bank[0:DH, :], ACT.Copy)
                        n = H_I if what == "kIwI" else DH
                        last = act.activation(vT[0:n, :], bank[DH:DH + n, :], ACT.Copy)
                    elif what == "qI":
                        act.activation(q_i[0:DH, 2 * p, cut], bank[0:DH, :], ACT.Copy, scale=DH ** -0.5)
                        last = act.activation(q_i[DH:P, 2 * p + 1, cut], bank[DH:P, :], ACT.Copy, scale=DH ** -0.5)
                    elif what == "k":
                        for a in range(2):
                            for half in range(2):
                                last = act.activation(qk[DH * half:DH * half + DH, K_SLOT[p % 2] + a, cut],
                                                      bank[DH * a:DH * a + DH, :], ACT.Copy)
                    elif what == "v":
                        last = act.activation(vT[:, :], bank[:, :], ACT.Copy)
                    elif what == "q" and PAIRS[p][0] == "M":
                        last = act.activation(q_m[:, cut], bank[:, :], ACT.Copy, scale=query_scale(p, 0))
                    elif what == "q":
                        for a in range(2):
                            rows = slice(DH * a, DH * a + DH)
                            last = act.activation(qk[rows, a, cut], bank[rows, :], ACT.Copy, scale=query_scale(p, a))
                    else:
                        if p == NP - 1:
                            act.wait_ge(pv_done, CHUNK0[(NP - 3) * NT])
                        elif p >= 1:
                            act.wait_ge(og_stored[b], 16 * p)
                        last = act.activation(gates(p)[:, cut], bank[:, :], ACT.Copy)
                last.then_inc(j_free, 1)
                if kind == "w" and W_TILES[w][0] == "gate" and b == 1:
                    act.wait_ge(j_free, m + 1)
                    act.activation(gates(W_TILES[w][1]), gates(W_TILES[w][1]), ACT.Silu).then_inc(gate_ready, 1)

            square_sums(range(0, MT))
            root(0, 0, MT)
            split_hi(0)
            square_sums(range(MT, MT + 4))
            root(1, MT, MT + 4)

            def high(u):
                r, b = u // 2, u % 2
                act.wait_ge(turned, u + 1)
                src = turn_banks[u % 6].rearrange("p (k t) -> p k t", k=4)
                if r < MT:
                    dst = memT[:, 4 * b:4 * b + 4, P * r:P * r + P]
                else:
                    dst = h_hi[:, 4 * b:4 * b + 4, P * (r - MT):P * (r - MT) + P]
                act.activation(dst, src, ACT.Copy).then_inc(hi_ready, 1)

            for u in range(2 * MT):
                high(u)
            square_sums(range(MT + 4, MT + NT))
            root(2, MT + 4, MT + NT)
            m = 0
            for _ in range(5):
                evacuate(m)
                m += 1
            for u in range(2 * MT, 2 * (MT + NT)):
                high(u)
            for w in range(W_OF["q", 0]):
                split_hi(w + 1)
                for _ in range(2 if w else 4):
                    evacuate(m)
                    m += 1
            split_hi(PRE_W - 1)
            for u, (i, h) in enumerate(IDX_UNITS):
                if h == 0 and i - FIRST_TOPK < len(PRE_PAIR_HALVES):
                    evacuate(m)
                    m += 1
                act.wait_ge(idx_scored, u + 1)
                if u >= 4:
                    act.wait_ge(idx_added, u - 3)
                n = P * (i + 1)
                act.activation(relu[u % 4][:, 0:n], s_ps[u % 2][:, 0:n], ACT.Relu).then_inc(relu_ready, 1)
            def mix_hi(t):
                act.wait_ge(mixed_in[t % 2], 16 * (t // 2 + 1))
                if t >= 2:
                    act.wait_ge(out_done, 2 * (t - 1))
                act.activation(w_hl[:, t % 2, 0, 0:NP - 1, :], mixed[t % 2], ACT.Copy).then_inc(mix_hi_ready, 1)

            def last_hi(t):
                act.wait_ge(og_ready, 2 * (NP - 1) + t // EARLY + 1)
                act.activation(w_hl[:, t % 2, 0, NP - 1, :], gates(NP - 1)[:, P * t:P * t + P],
                               ACT.Copy).then_inc(last_hi_ready, 1)

            next_w = PRE_W

            def copy_probT(s, c):
                g = CHUNK0[s] + c
                act.wait_ge(pt_done[0], g + 1)
                if g >= 2:
                    act.wait_ge(pv_done, g - 1)
                n = len(chunks(s)[c])
                act.activation(probT[:, g % 2, 0, 0:n, :], pt_ps[0][:, 0:n, :], ACT.Copy).then_inc(pt_ready[0], 1)

            def exponent(s, a):
                p, i = pair_of_step(s)
                n = P * key_tiles(s)
                act.wait_ge(biased[a], s + 1)
                act.activation(prob[:, a, s % 2, 0:n], prob[:, a, s % 2, 0:n], ACT.Exp, scale=-1.0,
                               bias=nmax[:, a, s % 2:s % 2 + 1],
                               accum_out=lsum[:, p % 2, i, a:a + 1]).then_inc(prob_ready[a], 1)

            for s in range(STEPS + 1):
                if s < STEPS and v_turn_of_step(s):
                    evacuate(m)
                    m += 1
                if s >= 1:
                    copy_probT(s - 1, 0)
                if s < STEPS:
                    exponent(s, 0)
                    exponent(s, 1)
                if s >= 1 and len(chunks(s - 1)) == 2:
                    copy_probT(s - 1, 1)
                if s < STEPS:
                    p, i = pair_of_step(s)
                    while next_w < min(coming(s) + 2, N_W):
                        split_hi(next_w)
                        next_w += 1
                    if projection_of_step(s):
                        evacuate(m)
                        m += 1
                    for n in wo_of_step(s):
                        act.wait_ge(wo_in[n % WO_ROOMS], 16 * (n // WO_ROOMS + 1))
                        act.wait_ge(j_done, projected(N_W - 1))
                        act.activation(wo_hi[:, n, :], wo_raw[n % WO_ROOMS], ACT.Copy).then_inc(wo_hi_ready, 1)
                if s == STEPS - 4:
                    act.wait_ge(j_done, projected(N_W - 1))
                    mix_hi(0)
                    mix_hi(1)
                if s == STEPS - 3:
                    last_hi(0)
                    last_hi(1)
                if s in (STEPS - 2, STEPS - 1):
                    mix_hi(s - STEPS + 4)
                    last_hi(s - STEPS + 4)
            assert m == len(uses)

            def square_row(t):
                act.wait_ge(y_added, 2 * t + 2)
                if t >= 1:
                    act.wait_ge(ysq_ready, t)
                act.activation(sq_junk, y_rows[t], ACT.Square, accum_out=stat[:, 0, t:t + 1]).then_inc(ysq_ready, 1)

            def y_root(n, a, b):
                act.wait_ge(yvar_ready, n + 1)
                act.activation(stat[:, 2, a:b], stat[:, 1, a:b], ACT.Sqrt).then_inc(yroot_ready, 1)

            for t in range(NT):
                if t + 4 < EARLY + 2 or t >= EARLY and t + 2 < NT:
                    ahead = t + 4 if t < EARLY else t + 2
                    mix_hi(ahead)
                    last_hi(ahead)
                square_row(t)
                if t >= EARLY - 1:
                    y_root(t - EARLY + 1, 0 if t < EARLY else t, t + 1)

        @block.vector
        def _(dve):
            chain = [0]

            def link(ins):
                chain[0] += 1
                ins.then_inc(dve_seq, 1)
                dve.wait_ge(dve_seq, chain[0])

            def variance(a, b, ready):
                dve.tensor_scalar(stat[:, 1, a:b], stat[:, 0, a:b], 1.0 / D, EPS, ALU.mult, ALU.add).then_inc(ready, 1)

            def inverse_root(a, b):
                v, r, y, t = (stat[:, n, a:b] for n in range(1, 5))
                link(dve.reciprocal(y, r))
                link(dve.tensor_tensor(t, y, y, ALU.mult))
                link(dve.tensor_tensor(t, t, v, ALU.mult))
                link(dve.tensor_scalar(t, t, -0.5, 1.5, ALU.mult, ALU.add))
                link(dve.tensor_tensor(y, y, t, ALU.mult))

            scaled = [0]

            def scale_tile(r):
                if scaled[0] >= 2:
                    dve.wait_ge(turned, 2 * (scaled[0] - 1))
                dve.scalar_tensor_tensor(out=x_scaled[r % 2], in0=x_raw[r], scalar=stat[:, 3, r:r + 1],
                                         in1=(gm_row if r < MT else g_row), op0=ALU.mult,
                                         op1=ALU.mult).then_inc(x_ready, 1)
                scaled[0] += 1

            def low(u):
                r, b = u // 2, u % 2
                dve.wait_ge(hi_ready, u + 1)
                at = (slice(None), slice(4 * b, 4 * b + 4), slice(P * (r - MT), P * (r - MT) + P))
                dve.tensor_tensor(h_lo[at], turn_banks[u % 6].rearrange("p (k t) -> p k t", k=4),
                                  h_hi[at].bitcast(F32), ALU.subtract).then_inc(lo_ready, 1)

            batches = ((0, MT), (MT, MT + 4), (MT + 4, MT + NT))
            for n, (a, b) in enumerate(batches):
                dve.wait_ge(squares_ready, b)
                variance(a, b, var_ready)
                dve.wait_ge(root_ready, n + 1)
                inverse_root(a, b)
                if n == 0:
                    dve.wait_ge(rows_in, 32)
                if n < 2:
                    for r in range(a, a + 2):
                        scale_tile(r)
            for r in range(MT + 2, MT + NT):
                low(2 * (r - 2))
                low(2 * (r - 2) + 1)
                scale_tile(r)
            low(2 * (MT + NT - 2))
            low(2 * (MT + NT - 2) + 1)
            low(2 * (MT + NT - 1))
            low(2 * (MT + NT - 1) + 1)

            def split_low(m):
                _, w, b = uses[m]
                bank = bank_of(m)
                what, p, _ = W_TILES[w]
                cut = slice(HALF * b, HALF * b + HALF)
                dve.wait_ge(j_free, m + 1)

                def part(dst, rows, hi, scale=1.0):
                    return dve.scalar_tensor_tensor(out=dst, in0=bank[rows, :], scalar=scale, in1=hi.bitcast(F32),
                                                    op0=ALU.mult, op1=ALU.subtract)

                lower, upper = slice(0, DH), slice(DH, P)
                if what in ("kIwI", "kvB"):
                    part(kk_b[lower, 1, cut], lower, kk_b[lower, 0, cut])
                    last = part(kk_b[upper, 1, cut], lower, kk_b[lower, 0, cut])
                elif what == "k":
                    slot = K_SLOT[p % 2]
                    part(qk[lower, slot + 2, cut], lower, qk[lower, slot, cut])
                    last = part(qk[upper, slot + 2, cut], upper, qk[upper, slot + 1, cut])
                else:
                    slot = 2 * p if what == "qI" else 0
                    scale = [DH ** -0.5 if what == "qI" else query_scale(p, a) for a in range(2)]
                    part(qk[upper, slot, cut], lower, qk[lower, slot, cut], scale[0])
                    last = part(qk[lower, slot + 1, cut], upper, qk[upper, slot + 1, cut], scale[1])
                last.then_inc(j_split, 1)

            for m in range(use_number["w", W_OF["q", 0], 0]):
                if is_split(m):
                    split_low(m)
            for u, (i, h) in enumerate(IDX_UNITS):
                if u == 0:
                    dve.wait_ge(j_free, use_number[("wturn", 0, 1)] + 1)
                dve.wait_ge(relu_ready, u + 1)
                n = P * (i + 1)
                wt = w_i[:, i, h:h + 1]
                if h == 0:
                    dve.tensor_scalar(x_slice(i), relu[u % 4][:, 0:n], wt, None, ALU.mult).then_inc(idx_added, 1)
                else:
                    dve.wait_ge(idx_added, u)
                    dve.scalar_tensor_tensor(out=x_slice(i), in0=relu[u % 4][:, 0:n], scalar=wt, in1=x_slice(i),
                                             op0=ALU.mult, op1=ALU.add).then_inc(idx_added, 1)
                if h == H_I - 1:
                    dve.wait_ge(idx_added, u + 1)
                    dve.tensor_reduce(reach[:, i - FIRST_TOPK:i - FIRST_TOPK + 1], x_slice(i), AX_X, ALU.max,
                                      apply_absolute_value=True).then_inc(reach_ready, 1)

            def choose(t, slot):
                xs, n = x_slice(t), P * (t + 1)
                level, step, count, extra, flag, late = (tk[:, c:c + 1] for c in (0, 1, 2, 3, 5, 4))
                some = picked[:, 0:n]
                if slot == 0:
                    if t > FIRST_TOPK:
                        dve.wait_ge(mask_ready, t - FIRST_TOPK)
                        dve.wait_ge(spoiled_any, t - FIRST_TOPK)
                    link(dve.tensor_copy(step, reach[:, t - FIRST_TOPK:t - FIRST_TOPK + 1]))
                    link(dve.memset(level, 0.0))
                elif slot <= HALVINGS:
                    if slot == 1 and t == (T - 2 * N_MEM) // P:
                        dve.wait_ge(pv_done, CHUNK0[2 * NT])
                    link(dve.tensor_scalar(some, xs, level, None, ALU.is_ge, ALU.add, accum_out=count))
                    link(dve.tensor_scalar(step, step, 0.5, None, ALU.mult))
                    link(dve.tensor_scalar(count, count, float(TOPK), 0.5, ALU.is_ge, ALU.subtract))
                    link(dve.tensor_scalar(count, count, 2.0, None, ALU.mult))
                    link(dve.scalar_tensor_tensor(out=level, in0=step, scalar=count, in1=level,
                                                  op0=ALU.mult, op1=ALU.add))
                elif slot == HALVINGS + 1:
                    link(dve.scalar_tensor_tensor(out=level, in0=step, scalar=-1.01, in1=level,
                                                  op0=ALU.mult, op1=ALU.add))
                    link(dve.tensor_scalar(some, xs[:, ::-1], level, None, ALU.is_lt, ALU.add, accum_out=count))
                    link(dve.tensor_scalar(extra, count, -1.0, float(n - TOPK), ALU.mult, ALU.add))
                elif slot == HALVINGS + 2:
                    link(dve.scalar_tensor_tensor(out=some, in0=some, scalar=NEVER, in1=xs[:, ::-1],
                                                  op0=ALU.mult, op1=ALU.subtract))
                    link(dve.tensor_scalar(late, extra, 7.5, None, ALU.is_gt))
                    dve.scalar_tensor_tensor(out=flag, in0=extra, scalar=-0.5, in1=late,
                                             op0=ALU.is_lt, op1=ALU.add).then_inc(spoiled, 1)
                elif slot == HALVINGS + 3:
                    if t == FIRST_TOPK:
                        dve.wait_ge(eight_ready, 1)
                    link(dve.max(cut8[:, 0, :], some))
                    link(dve.scalar_tensor_tensor(out=cut8[:, 0, :], in0=eight[:, :], scalar=extra,
                                                  in1=cut8[:, 0, :], op0=ALU.is_lt, op1=ALU.mult))
                    link(dve.tensor_scalar(cut8[:, 1, :], eight[:, :], extra, NEVER, ALU.is_ge, ALU.mult))
                    link(dve.tensor_tensor(cut8[:, 2, :], cut8[:, 0, :], cut8[:, 1, :], ALU.add))
                elif slot == HALVINGS + 4:
                    link(dve.match_replace(out=some, in_to_replace=cut8[:, 2, :], in_values=some, imm_value=NEVER))

            def settle(t):
                xs, n = x_slice(t), P * (t + 1)
                dve.wait_ge(spoiled_any, t - FIRST_TOPK + 1)
                rows = dve.value_load(failed[0:1, 0:1], min_val=0, max_val=P)
                with dve.If(rows > 0):
                    with dve.Fori(0, ROUNDS):
                        dve.max(cut8[:, 0, :], xs)
                        dve.drain()
                        dve.match_replace(out=xs, in_to_replace=cut8[:, 0, :], in_values=xs, imm_value=NEVER)
                        dve.drain()
                    dve.tensor_scalar(picked[:, 0:n], xs[:, ::-1], -2e38, NEVER, ALU.is_ge, ALU.mult)
                dve.drain().then_inc(topk_done, 1)

            def choose_slots(p, slots):
                for slot in slots:
                    choose(IDX_TILES[p], slot)

            def add_bias(s, a):
                p, i = pair_of_step(s)
                g = PAIRS[p][0]
                n = P * key_tiles(s)
                dve.wait_ge(scored[a], s + 1)
                if s >= 2:
                    dve.wait_ge(pt_done[a], CHUNK0[s - 1])
                low_out = nmax[:, a, s % 2:s % 2 + 1]
                dst = prob[:, a, s % 2, 0:n]
                if g == "M":
                    dve.tensor_scalar(dst, s_ps[a][:, 0:n], 1.0, 3e38, ALU.mult, ALU.min,
                                      accum_out=low_out).then_inc(biased[a], 1)
                    return
                if g == "A":
                    if i == 0:
                        dve.wait_ge(bias_in, 32 * (p - 1))
                    table, scale = bias[:, a, T - n:T], 1.0
                else:
                    if i == 0:
                        dve.wait_ge(consts_in, 16)
                    if i >= FIRST_TOPK:
                        dve.wait_ge(mask_ready, i - FIRST_TOPK + 1)
                    table, scale = dist_of(i), slope_of(p, a)
                dve.tensor_tensor_reduce(dst, s_ps[a][:, 0:n], table, scale, 3e38, ALU.add, ALU.min,
                                         low_out).then_inc(biased[a], 1)

            def copy_probT(s, c):
                g = CHUNK0[s] + c
                dve.wait_ge(pt_done[1], g + 1)
                if g >= 2:
                    dve.wait_ge(pv_done, g - 1)
                n = len(chunks(s)[c])
                dve.tensor_copy(probT[:, g % 2, 1, 0:n, :], pt_ps[1][:, 0:n, :]).then_inc(pt_ready[1], 1)

            groups = [0]

            def invert_sums(p, g):
                for a in range(2):
                    dve.wait_ge(prob_ready[a], p * NT + 4 * g + 4)
                inverse = lsum[:, p % 2, 4 * g:4 * g + 4, :]
                link(dve.reciprocal(inverse, inverse))
                dve.tensor_copy(linv[:, :, :, :], inverse.unsqueeze(3).broadcast_to([P, 4, 2, DH])).then_inc(linv_ready, 1)
                groups[0] += 1

            def finish_group(p, g):
                dve.wait_ge(gate_ready, p + 1)
                dve.wait_ge(linv_turned, groups[0])
                cut = slice(HALF * g, HALF * g + HALF)
                dve.tensor_tensor(gates(p)[:, cut], pt_ps[0][:, :, :].rearrange("p a b -> p (a b)"),
                                  gates(p)[:, cut], ALU.mult).then_inc(linv_used, 1)
                dve.wait_ge(linv_used, groups[0])
                dve.wait_ge(pv_done, CHUNK0[p * NT + 4 * g + 4])
                dve.tensor_tensor(gates(p)[:, cut], o_ps[:, :], gates(p)[:, cut], ALU.mult).then_inc(og_ready, 1)

            def add_residual(t, b):
                bank = j_ps[:, :] if t < EARLY else s_ps[t % 2][:, HALF * b:HALF * b + HALF]
                row = y_rows[t][:, HALF * b:HALF * b + HALF]
                dve.wait_ge(out_done, 2 * t + b + 1)
                dve.wait_ge(xr_in[t], 16)
                dve.tensor_tensor(row, bank, row, ALU.add).then_inc(y_added, 1)

            for s in range(STEPS + 1):
                p, i = pair_of_step(s)
                early = EARLY_OUT.get(s, (None, None, None))
                if s < STEPS:
                    if i == 0 and p < len(IDX_TILES):
                        dve.wait_ge(idx_masked, p + 1)
                    add_bias(s, 0)
                    add_bias(s, 1)
                if s >= 1:
                    copy_probT(s - 1, 0)
                if s >= 1 and (s - 1) % 4 == 3:
                    invert_sums(pair_of_step(s - 1)[0], (s - 1) % NT // 4)
                if s < STEPS:
                    if i == 0 and 1 <= p <= len(IDX_TILES):
                        settle(IDX_TILES[p - 1])
                    if i >= 1 and p < len(IDX_TILES):
                        choose_slots(p, CHOICE_SLOTS[2 * i - 2])
                if early[0]:
                    add_residual(*early[0])
                if s >= 1 and len(chunks(s - 1)) == 2:
                    copy_probT(s - 1, 1)
                if early[1]:
                    add_residual(*early[1])
                if s < STEPS and i >= 1 and p < len(IDX_TILES):
                    choose_slots(p, CHOICE_SLOTS[2 * i - 1])
                if s >= 1 and (s - 1) % 4 == 3:
                    finish_group(pair_of_step(s - 1)[0], (s - 1) % NT // 4)
                if early[2]:
                    add_residual(*early[2])
                if s < STEPS and projection_of_step(s) and is_split(use_number["w", *projection_of_step(s)]):
                    split_low(use_number["w", *projection_of_step(s)])

            def final_norm(n, a, b):
                dve.wait_ge(ysq_ready, b)
                variance(a, b, yvar_ready)
                dve.wait_ge(yroot_ready, n + 1)
                inverse_root(a, b)
                for t in range(a, b):
                    dve.scalar_tensor_tensor(out=y_rows[t], in0=y_rows[t], scalar=stat[:, 3, t:t + 1], in1=gf_row,
                                             op0=ALU.mult, op1=ALU.mult).then_inc(y_final, 1)

            dve.wait_ge(gf_in, 16)
            final_norm(0, 0, EARLY)
            for t in range(EARLY, NT):
                add_residual(t, 0)
                add_residual(t, 1)
                final_norm(t - EARLY + 1, t, t + 1)

        @block.tensor
        def _(pe):
            pe.wait_ge(ident_ready, 2)

            def turn(u):
                r, b = u // 2, u % 2
                pe.wait_ge(x_ready, r + 1)
                if u >= 6:
                    pe.wait_ge(hi_ready, u - 5)
                if u - 6 >= 2 * MT:
                    pe.wait_ge(lo_ready, u - 5 - 2 * MT)
                for c in range(4):
                    k = 4 * b + c
                    last = pe.transpose(turn_banks[u % 6][:, P * c:P * c + P], x_scaled[r % 2][:, P * k:P * k + P],
                                        ident[:, :])
                last.then_inc(turned, 1)

            m = 0

            def fill(m, ks=range(KD)):
                kind, w, b = uses[m]
                bank = bank_of(m)
                if free_before(m) > 0 and ks[0] == 0:
                    wait_evacuated(pe, free_before(m) - 1)
                if kind == "mem":
                    pe.wait_ge(wm_in[w % 2], 16 * (w // 2 + 1))
                    for k in range(KD):
                        last = pe.matmul(bank[:, 0:N_MEM], wm_raw[:, w % 2, k, :], memT[:, k, :],
                                         start=(k == 0), stop=(k == KD - 1))
                elif kind == "memturn":
                    pe.wait_ge(j_free, m)
                    for t in range(MT):
                        for f in range(2):
                            at = N_MEM * t + P * f
                            last = pe.transpose(bank[:, at:at + P], vmT[:, f, P * t:P * t + P], ident[:, :])
                elif kind == "wturn":
                    pe.wait_ge(j_free, m)
                    for c in range(4):
                        last = pe.transpose(bank[:, H_I * c:H_I * c + H_I], vT[0:H_I, P * c:P * c + P],
                                            ident[0:H_I, 0:H_I])
                elif kind == "vturn":
                    n = P if PAIRS[w][0] == "A" else DH
                    for c in range(4):
                        last = pe.transpose(bank[:, n * c:n * c + n], vT[0:n, P * c:P * c + P], ident[0:n, 0:n])
                else:
                    if ks[0] == 0:
                        pe.wait_ge(w_lo_ready, w + 1)
                    n = width(w)
                    hi, lo = w_hl[:, w % 2, 0], w_hl[:, w % 2, 1]
                    passes = [(hi, h_hi), (hi, h_lo), (lo, h_hi)]
                    for k in ks:
                        for q, (a, c) in enumerate(passes):
                            last = pe.matmul(bank[0:n, :], a[:, k, 0:n], c[:, k, HALF * b:HALF * b + HALF],
                                             start=(k == 0 and q == 0), stop=(k == KD - 1 and q == 2))
                if kind != "w" or ks[-1] == KD - 1:
                    last.then_inc(j_done, 1)

            for u in range(2 * MT):
                turn(u)
            pe.wait_ge(hi_ready, 2 * MT)
            for _ in range(5):
                fill(m)
                m += 1
            for u in range(2 * MT, 2 * (MT + NT)):
                turn(u)
            pe.wait_ge(lo_ready, 2 * NT)
            while uses[m] != ("w", *PRE_PAIR_HALVES[0]):
                fill(m)
                m += 1
            def product(bank, q, k_hi, k_lo, a, i):
                rows = slice(DH * a, DH * a + DH)
                tile = slice(P * i, P * i + P)
                for c in range(0, P * (i + 1), HALF):
                    keys = slice(c, min(c + HALF, P * (i + 1)))
                    pe.matmul(bank[:, keys], q[:, tile], k_hi[:, keys], start=True, stop=False)
                    last = pe.matmul(bank[:, keys], q[rows, tile], k_lo[rows, keys], start=False, stop=True)
                return last

            for u, (i, h) in enumerate(IDX_UNITS):
                if h == 0 and i - FIRST_TOPK < len(PRE_PAIR_HALVES):
                    fill(m)
                    m += 1
                if u == 0:
                    wait_evacuated(pe, use_number["w", W_OF["q", 0], 0] - 1)
                if u >= 2:
                    pe.wait_ge(relu_ready, u - 1)
                product(s_ps[u % 2], q_i[:, h, :], kk_i[:, 0, :], kk_i[:, 1, :], h % 2, i).then_inc(idx_scored, 1)

            def scores(s, a):
                p, i = pair_of_step(s)
                g = PAIRS[p][0]
                if i % 4 == 0 and a == 0:
                    wait_evacuated(pe, use_number["w", W_OF["q", p], i // 4])
                if s == 0:
                    pe.wait_ge(j_free, n_pre)
                    pe.wait_ge(relu_ready, len(IDX_UNITS))
                else:
                    pe.wait_ge(biased[a], s)
                if g == "M":
                    rows = slice(DH * a, DH * a + DH)
                    last = pe.matmul(s_ps[a][:, 0:N_MEM], q_m[rows, P * i:P * i + P], k_m[rows, PAIRS[p][1], :],
                                     start=True, stop=True)
                elif g == "A":
                    slot = K_SLOT[p % 2]
                    last = product(s_ps[a], qk[:, a, :], qk[:, slot + a, :], qk[:, slot + 2, :], a, i)
                else:
                    last = product(s_ps[a], qk[:, a, :], kk_b[:, 0, :], kk_b[:, 1, :], a, i)
                last.then_inc(scored[a], 1)

            def turn_prob(s, c):
                g = CHUNK0[s] + c
                for a in range(2):
                    pe.wait_ge(prob_ready[a], s + 1)
                    if g >= 1:
                        pe.wait_ge(pt_ready[a], g)
                    if a == 0 and s // 4 >= 1:
                        pe.wait_ge(linv_used, s // 4)
                    for n, k in enumerate(chunks(s)[c]):
                        last = pe.transpose(pt_ps[a][:, n, :], prob[:, a, s % 2, P * k:P * k + P], ident[:, :])
                    last.then_inc(pt_done[a], 1)

            def values(s, c):
                p, i = pair_of_step(s)
                g = CHUNK0[s] + c
                pr, j = PAIRS[p][0], PAIRS[p][1]
                for a in range(2):
                    pe.wait_ge(pt_ready[a], g + 1)
                if i % 4 == 0 and c == 0 and s >= 4:
                    pe.wait_ge(og_ready, s // 4)
                at = slice(P * (i % 4), P * (i % 4) + P)
                nk = key_tiles(s)
                for n, k in enumerate(chunks(s)[c]):
                    for a in range(2):
                        if pr == "A":
                            v = v_sb[:, p % 2, k, DH * a:DH * a + DH]
                        elif pr == "B":
                            v = v_b[:, k, :]
                        else:
                            v = v_m[:, k, P * j + DH * a:P * j + DH * a + DH]
                        last = pe.matmul(o_ps[DH * a:DH * a + DH, at], v, probT[:, g % 2, a, n, :],
                                         start=(k == 0), stop=(k == nk - 1))
                last.then_inc(pv_done, 1)

            def turn_sums(s):
                p, i = pair_of_step(s)
                pe.wait_ge(linv_ready, s // 4 + 1)
                pe.wait_ge(pt_ready[0], CHUNK0[s + 1])
                for c in range(4):
                    last = pe.transpose(pt_ps[0][:, c, :], linv[:, c, :, :].rearrange("p a f -> p (a f)"), ident[:, :])
                last.then_inc(linv_turned, 1)

            def project_out(t, b):
                if (t, b) == (0, 0):
                    wait_evacuated(pe, len(uses) - 1)
                    pe.wait_ge(wo_hi_ready, NP)
                    pe.wait_ge(wo_lo_ready, NP)
                elif t < EARLY:
                    pe.wait_ge(y_added, 2 * t + b)
                elif t < EARLY + 2:
                    pe.wait_ge(biased[t % 2], STEPS)
                else:
                    pe.wait_ge(y_added, 2 * (t - 2) + b + 1)
                if b == 0:
                    pe.wait_ge(mix_lo_ready, t + 1)
                    pe.wait_ge(last_lo_ready, t + 1)
                hi, lo = w_hl[:, t % 2, 0], w_hl[:, t % 2, 1]
                passes = [(hi, wo_hi), (hi, wo_lo), (lo, wo_hi)]
                cut = slice(HALF * b, HALF * b + HALF)
                bank = j_ps[:, :] if t < EARLY else s_ps[t % 2][:, cut]
                for p in range(NP):
                    for q, (a, c) in enumerate(passes):
                        last = pe.matmul(bank, a[:, p, :], c[:, p, cut],
                                         start=(p == 0 and q == 0), stop=(p == NP - 1 and q == 2))
                last.then_inc(out_done, 1)

            for s in range(STEPS + 1):
                early = EARLY_OUT.get(s, (None, None, None))
                if s < STEPS:
                    scores(s, 0)
                    scores(s, 1)
                    if v_turn_of_step(s):
                        fill(m)
                        m += 1
                if s >= 1:
                    turn_prob(s - 1, 0)
                two = s >= 1 and len(chunks(s - 1)) == 2
                if s < STEPS and projection_of_step(s):
                    fill(m, range(0, KD // 2 if two else KD))
                if early[0]:
                    project_out(*early[0])
                if s >= 1:
                    values(s - 1, 0)
                if two:
                    turn_prob(s - 1, 1)
                if early[1]:
                    project_out(*early[1])
                if s < STEPS and projection_of_step(s):
                    if two:
                        fill(m, range(KD // 2, KD))
                    m += 1
                if two:
                    values(s - 1, 1)
                if s >= 1 and (s - 1) % 4 == 3:
                    turn_sums(s - 1)
                if early[2]:
                    project_out(*early[2])
            assert m == len(uses)

            for t in range(EARLY, NT):
                for b in range(2):
                    project_out(t, b)


def distance_table():
    d = np.arange(P)[:, None] + (T - P) - np.arange(T)[None, :]
    return d, np.where(d >= 0, d, BIG).astype(np.float32)


def window_tables():
    d, _ = distance_table()
    count = np.zeros(d.shape)
    for window, dilation in ((128, 1), (512, 4), (2048, 16)):
        count += (d >= 0) & (d % dilation == 0) & (d <= window)
    heads = []
    for h in range(H_A):
        slope = 2.0 ** (-8.0 * (h + 1) / H_A)
        heads.append(np.where(count > 0, slope * d - np.log(np.maximum(count, 1)), BIG))
    return np.stack(heads).astype(np.float32)


_INS = ["x", "mem", "g_in", "g_mem", "w_in", "w_mem_kv", "w_out", "g_final"]


def kernel(**inputs):
    import numpy as _np
    import concourse.bacc as _bacc
    from concourse import mybir as _mybir
    from concourse.bass_utils import run_bass_kernel_spmd as _run

    nc = _bacc.Bacc("TRN2", target_bir_lowering=False, num_devices=1)
    arrays, args = {}, []
    tables = {"dist_tab": distance_table()[1], "a_tab": window_tables()}
    for name in _INS + list(tables):
        a = _np.ascontiguousarray(tables[name] if name in tables else inputs[name])
        arrays[f"in_{name}_dram"] = a
        args.append(nc.dram_tensor(f"in_{name}_dram", a.shape, _mybir.dt.from_np(a.dtype), kind="ExternalInput").ap())
    args.append(nc.dram_tensor("out_0_dram", (1, T, D), F32, kind="ExternalOutput").ap())
    build_program(nc, *args)
    r = _run(nc, [arrays], core_ids=[0])
    return r.results[0]["out_0_dram"]
```

```python
import math
from contextlib import ExitStack

import numpy as np

import concourse.bass as bass
from concourse import mybir

F32 = mybir.dt.float32
F32R = mybir.dt.float32r
ALU = mybir.AluOpType
ACT = mybir.ActivationFunctionType
AX_X = mybir.AxisListType.X

P = 128
T = 1024
D = 1024
KD = D // P
NT = T // P
N_MEM = 256
MT = N_MEM // P
DH = 64
HALF = 512
H_A, H_B, H_M, H_I = 8, 4, 4, 8
TOPK = 256
FIRST_TOPK = TOPK // P
EPS = 1e-6
BIG = 1e30

C_QA, C_KA, C_VA = 0, 512, 1024
C_QB = 1536
C_KB = C_QB + H_B * DH
C_VB = C_KB + DH
C_QM = C_VB + DH
C_GATE = C_QM + H_M * DH
C_QI = C_GATE + 1024
C_KI = C_QI + H_I * DH
C_WI = C_KI + DH

PAIRS = [("M", 0, 6), ("M", 1, 7), ("A", 0, 0), ("A", 1, 1), ("A", 2, 2), ("A", 3, 3), ("B", 0, 4), ("B", 1, 5)]
NP = len(PAIRS)
STEPS = NP * NT


GATES_WITH = {NP - 3: [NP - 3, NP - 1], NP - 1: []}


def w_tiles():
    def q_tile(p):
        g, j, _ = PAIRS[p]
        return "q", p, [({"A": C_QA, "B": C_QB, "M": C_QM}[g] + P * j, P)]

    out = [("kIwI", None, [(C_KI, DH), (C_WI, H_I)])]
    out += [("qI", j, [(C_QI + P * j, P)]) for j in range(H_I // 2)]
    out += [q_tile(0)]
    for p, (g, j, f) in enumerate(PAIRS):
        follows = PAIRS[p + 1][:2] if p + 1 < NP else None
        if follows and follows[0] == "A":
            out += [("k", p + 1, [(C_KA + P * follows[1], P)])]
        if follows == ("B", 0):
            out += [("kvB", p + 1, [(C_KB, DH), (C_VB, DH)])]
        out += [("gate", q, [(C_GATE + P * PAIRS[q][2], P)]) for q in GATES_WITH.get(p, [p])]
        if follows and follows[0] == "A":
            out += [("v", p + 1, [(C_VA + P * follows[1], P)])]
        if follows:
            out += [q_tile(p + 1)]
    return out


W_TILES = w_tiles()
W_OF = {(what, p): n for n, (what, p, _) in enumerate(W_TILES)}
N_W = len(W_TILES)
PRE_W = W_OF["gate", 0] + 1
SLOT = {"k": 0, "kvB": 0, "gate": 2, "v": 4, "q": 6}


def slope_of(p, a):
    return 2.0 ** (-8.0 * (2 * PAIRS[p][1] + a + 1) / H_B)


def query_scale(p, a):
    return -(DH ** -0.5) / (slope_of(p, a) if PAIRS[p][0] == "B" else 1.0)


LAST_GATE_AT = [(NP - 3, 4), (NP - 3, 5)]


def width(w):
    return sum(n for _, n in W_TILES[w][2])


def pair_of_step(s):
    return s // NT, s % NT


def key_tiles(s):
    p, i = pair_of_step(s)
    return MT if PAIRS[p][0] == "M" else i + 1


def chunks(s):
    n = key_tiles(s)
    return [range(c, min(c + 4, n)) for c in range(0, n, 4)]


CHUNK0 = [sum(len(chunks(q)) for q in range(s)) for s in range(STEPS + 1)]


def projection_of_step(s):
    p, i = pair_of_step(s)
    for what, at in SLOT.items():
        w = W_OF.get((what, p if what == "gate" else p + 1))
        if w is not None and w >= PRE_W and i in (at, at + 1) and (what, p) != ("gate", NP - 1):
            return w, i - at
    if (p, i) in LAST_GATE_AT:
        return W_OF["gate", NP - 1], LAST_GATE_AT.index((p, i))
    return None


def coming(s):
    return min([projection_of_step(q)[0] for q in range(s, STEPS) if projection_of_step(q)], default=N_W)


WO_PER_STEP = [3, 2, 2, 1]
WO_ROOMS = 3
EARLY = NT // 2
EARLY_OUT = {STEPS - 3: (None, (0, 0), None), STEPS - 2: ((0, 1), (1, 0), None),
             STEPS - 1: ((1, 1), (2, 0), None), STEPS: ((2, 1), (3, 0), (3, 1))}


def wo_of_step(s):
    at = s - (STEPS - NT)
    return range(sum(WO_PER_STEP[:at]), sum(WO_PER_STEP[:at + 1])) if 0 <= at < len(WO_PER_STEP) else range(0)


def v_turn_of_step(s):
    if s == 0 or projection_of_step(s - 1) is None:
        return None
    w, b = projection_of_step(s - 1)
    return (W_TILES[w][1], b) if W_TILES[w][0] in ("v", "kvB") else None


V_TURNS = [v_turn_of_step(s) for s in range(STEPS) if v_turn_of_step(s)]


def v_turns_before(p, b):
    return V_TURNS.index((p, b))


IDX_TILES = list(range(FIRST_TOPK, NT))
IDX_UNITS = [(i, h) for n in range(0, len(IDX_TILES), 2) for h in range(H_I) for i in IDX_TILES[n:n + 2]]
X_OFF = {i: sum(P * (q + 1) for q in range(FIRST_TOPK, i)) for i in IDX_TILES}
X_COLS = sum(P * (q + 1) for q in IDX_TILES)
PRE_PAIR_AT = len(IDX_UNITS) // 4
SPLIT_AT = {5 * PRE_PAIR_AT // 3: PRE_W, 10 * PRE_PAIR_AT // 3: PRE_W + 1}
PRE_PAIR_HALVES = [(W_OF[what, 0], b) for what in ("q", "gate") for b in range(2)]
K_SLOT = [2, 5]
ROUNDS = TOPK // 8
HALVINGS = 12
NEVER = -3e38
CHOICE_COUNTS = [2, 1, 2, 1, 2, 0, 2, 0, 2, 1, 2, 1, 1, 0]
CHOICE_SLOTS = [list(range(sum(CHOICE_COUNTS[:n]), sum(CHOICE_COUNTS[:n + 1]))) for n in range(2 * (NT - 1))]


def build_program(nc, x, mem, g_in, g_mem, w_in, w_mem, w_out, g_final, dist_tab, a_tab, out):
    with ExitStack() as ctx:
        def sb(name, shape, dt=F32):
            return ctx.enter_context(nc.sbuf_tensor(name, shape, dt))

        def sem(name):
            return ctx.enter_context(nc.semaphore(name))

        h_hi = sb("h_hi", [P, KD, T], F32R)
        h_lo = sb("h_lo", [P, KD, T], F32R)
        w_hl = sb("w_hl", [P, 2, 2, KD, P], F32R)
        w_raw = sb("w_raw", [P, KD, P])
        qk = sb("qk", [P, 8, T], F32R)
        kk_b = sb("kk_b", [P, 2, T], F32R)
        v_sb = sb("v_sb", [P, 2, NT, P])
        vT = sb("vT", [P, HALF])
        gate = sb("gate", [P, T])
        v_b = sb("v_b", [P, NT, DH])
        w_i = sb("w_i", [P, NT, H_I])
        bias = sb("bias", [P, 2, T])
        prob = sb("prob", [P, 2, 2, T])
        probT = sb("probT", [P, 2, 2, 4, P])
        idx = sb("idx", [P, X_COLS])
        mixed_dram = nc.dram_tensor("mixed_scratch", (NP - 1, P, T), F32, kind="Internal").ap()
        dist = sb("dist", [P, T])
        ident = sb("ident", [P, P])
        lsum = sb("lsum", [P, 2, NT, 2])
        linv = sb("linv", [P, 4, 2, DH])
        nmax = sb("nmax", [P, 2, 2])
        picked = sb("picked", [P, T])
        cut8 = sb("cut8", [P, 3, 8])
        eight = sb("eight", [P, 8])
        tk = sb("tk", [P, 8])
        reach = sb("reach", [P, len(IDX_TILES)])
        failed = sb("failed", [P, 1], mybir.dt.int32)
        stat = sb("stat", [P, 5, MT + NT])
        q_i = qk[:, :, :]
        kk_i = kk_b[:, :, :]
        x_rooms = [idx[:, 0:T], idx[:, T:2 * T], idx[:, 2 * T:3 * T], picked[:, :], idx[:, 3 * T:4 * T],
                   dist[:, :], bias[:, 1, :]]
        V_M_ROOM = 3
        x_raw = [x_rooms[r % len(x_rooms)] for r in range(MT + NT)]
        x_scaled = [prob[:, 0, 0, :], prob[:, 0, 1, :]]
        g_row, gm_row = prob[:, 1, 0, :], prob[:, 1, 1, :]
        q_m = v_sb[:, 1, :, :].rearrange("p t f -> p (t f)")
        memT = v_sb[:, :, :, :].rearrange("p a b c -> p (a b c)").rearrange("p (k m) -> p k m", k=KD)
        wm_raw = probT[:, :, :, :, :].rearrange("p a b c d -> p (a b c d)").rearrange("p (a k m) -> p a k m", a=2, k=KD)
        relu = [prob[:, 0, 0, :], prob[:, 0, 1, :], prob[:, 1, 0, :], prob[:, 1, 1, :]]
        w_iT = [vT[0:H_I, :], v_b[0:H_I, :, :].rearrange("p t f -> p (t f)")]
        k_m = bias[:, 0, 0:2 * N_MEM].rearrange("p (a m) -> p a m", a=2)
        v_m = picked[:, T - 2 * N_MEM:T].rearrange("p (t f) -> p t f", t=MT)
        vmT = vT[:, 0:2 * N_MEM].rearrange("p (a m) -> p a m", a=2)
        wo_hi, wo_lo = h_hi, h_lo
        wo_raw = [bias[:, 0, :], bias[:, 1, :], w_raw[:, :, :].rearrange("p k m -> p (k m)")]
        y_rows = [gate[:, :], v_sb[:, 1, :, :].rearrange("p t f -> p (t f)"), dist[:, :], picked[:, :],
                  prob[:, 0, 0, :], prob[:, 1, 0, :], prob[:, 0, 1, :], prob[:, 1, 1, :]]
        gf_row = idx[:, 0:T]
        sq_junk = qk[:, 2, :]
        mixed = [bias[:, b, 0:(NP - 1) * P].rearrange("p (q t) -> p q t", q=NP - 1) for b in range(2)]

        s_ps = [ctx.enter_context(nc.psum_tensor(f"s_ps{a}", [P, T], F32)) for a in range(2)]
        pt_ps = [ctx.enter_context(nc.psum_tensor(f"pt_ps{a}", [P, 4, P], F32)) for a in range(2)]
        o_ps = ctx.enter_context(nc.psum_tensor("o_ps", [P, HALF], F32))
        j_ps = ctx.enter_context(nc.psum_tensor("j_ps", [P, HALF], F32))
        turn_banks = [s_ps[0][:, 0:HALF], s_ps[0][:, HALF:T], s_ps[1][:, 0:HALF], s_ps[1][:, HALF:T],
                      pt_ps[0][:, :, :].rearrange("p a b -> p (a b)"), pt_ps[1][:, :, :].rearrange("p a b -> p (a b)")]

        x_in = [sem(f"x_in{r}") for r in range(MT + NT)]
        rows_in = [sem("rows_in0"), sem("rows_in1")]
        consts_in = sem("consts_in")
        ident_ready = sem("ident_ready")
        eight_ready = sem("eight_ready")
        squares_ready = sem("squares_ready")
        var_ready = sem("var_ready")
        root_ready = sem("root_ready")
        x_ready = sem("x_ready")
        turned = sem("turned")
        hi_ready = sem("hi_ready")
        lo_ready = sem("lo_ready")
        wm_in = [sem("wm_in0"), sem("wm_in1")]
        w_in_sem = sem("w_in_sem")
        w_hi_ready = sem("w_hi_ready")
        w_lo_ready = sem("w_lo_ready")
        j_done = sem("j_done")
        j_free = sem("j_free")
        j_split = sem("j_split")
        k_copied = sem("k_copied")
        v_turned = sem("v_turned")
        v_kept = sem("v_kept")
        gate_ready = sem("gate_ready")
        idx_scored = sem("idx_scored")
        relu_ready = sem("relu_ready")
        idx_added = sem("idx_added")
        reach_ready = sem("reach_ready")
        idx_masked = sem("idx_masked")
        spoiled = sem("spoiled")
        spoiled_any = sem("spoiled_any")
        topk_done = sem("topk_done")
        half_mask = sem("half_mask")
        mask_ready = sem("mask_ready")
        bias_in = sem("bias_in")
        scored = [sem("scored_a"), sem("scored_b")]
        biased = [sem("biased_a"), sem("biased_b")]
        prob_ready = [sem("prob_ready_a"), sem("prob_ready_b")]
        pt_done = [sem("pt_done_a"), sem("pt_done_b")]
        pt_ready = [sem("pt_ready_a"), sem("pt_ready_b")]
        pv_done = sem("pv_done")
        linv_ready = sem("linv_ready")
        linv_turned = sem("linv_turned")
        linv_used = sem("linv_used")
        og_ready = sem("og_ready")
        og_stored = [sem("og_stored0"), sem("og_stored1")]
        mixed_in = [sem("mixed_in0"), sem("mixed_in1")]
        wo_in = [sem(f"wo_in{n}") for n in range(WO_ROOMS)]
        wo_hi_ready = sem("wo_hi_ready")
        wo_lo_ready = [sem("wo_lo_ready0"), sem("wo_lo_ready1")]
        gf_in = sem("gf_in")
        xr_in = [sem(f"xr_in{t}") for t in range(NT)]
        mix_hi_ready = sem("mix_hi_ready")
        mix_lo_ready = sem("mix_lo_ready")
        last_hi_ready = sem("last_hi_ready")
        last_lo_ready = sem("last_lo_ready")
        out_done = sem("out_done")
        y_added = sem("y_added")
        ysq_ready = sem("ysq_ready")
        yvar_ready = sem("yvar_ready")
        yroot_ready = sem("yroot_ready")
        y_final = sem("y_final")
        stored = sem("stored")
        dve_seq = sem("dve_seq")

        x_t = x.rearrange("b (t p) d -> (b t) p d", p=P)
        mem_t = mem.rearrange("b (t p) d -> (b t) p d", p=P)
        w_k = w_in.rearrange("l (k p) c -> (l p) k c", p=P)
        wm_k = w_mem.rearrange("l (k p) c -> (l p) k c", p=P)
        wo_k = w_out.rearrange("l (f p) c -> (l f) p c", p=P)
        out_t = out.rearrange("b (t p) d -> (b t) p d", p=P)

        def gates(p):
            return gate[:, :] if p < NP - 1 else v_sb[:, 0, :, :].rearrange("p t f -> p (t f)")

        def dist_slice(i):
            return dist[:, T - P * (i + 1):T]

        def x_slice(i):
            return idx[:, X_OFF[i]:X_OFF[i] + P * (i + 1)]

        def dist_of(i):
            return dist_slice(i) if i < FIRST_TOPK else x_slice(i)

        uses = [("mem", w, 0) for w in range(4)] + [("memturn", 0, 0)]
        uses += [("w", w, b) for b in range(2) for w in range(2)] + [("wturn", 0, 0)]
        uses += [("w", w, b) for w in range(2, W_OF["q", 0]) for b in range(2)]
        uses += [("w", w, b) for w, b in PRE_PAIR_HALVES]
        n_pre = len(uses)
        steps_of_uses = [s for s in range(STEPS) if projection_of_step(s)]
        uses += [("w", *projection_of_step(s)) for s in steps_of_uses]
        use_number = {u: m for m, u in enumerate(uses)}
        key_uses = [m for m, (kind, w, _) in enumerate(uses) if kind == "w" and W_TILES[w][0] in ("kIwI", "k", "kvB")]
        bank_ids = []
        for m, (kind, _, _) in enumerate(uses):
            if m < n_pre:
                bank_ids.append(2 if kind == "wturn" else sum(b < 2 for b in bank_ids) % 2)
            else:
                s = steps_of_uses[m - n_pre]
                bank_ids.append(3 if key_tiles(s) <= 4 and s % 2 == 0 else 0)

        def bank_of(m):
            return [j_ps[:, :], o_ps[:, :], turn_banks[4], s_ps[0][:, HALF:T]][bank_ids[m]]

        def is_split(m):
            kind, w, _ = uses[m]
            what, p, _ = W_TILES[w] if kind == "w" else (None, None, None)
            return what in ("kIwI", "qI", "k", "kvB") or (what == "q" and PAIRS[p][0] != "M")

        def splits(m):
            return sum(is_split(q) for q in range(m))

        def free_before(m):
            return max([q + 1 for q in range(m) if bank_ids[q] == bank_ids[m]] + [n_pre if m >= n_pre else 0])

        def wait_evacuated(eng, m):
            eng.wait_ge(j_free, m + 1)
            if splits(m + 1):
                eng.wait_ge(j_split, splits(m + 1))

        def projected(w):
            return use_number[("w", w, 1)] + 1

        block = ctx.enter_context(nc.Block())

        @block.sync
        def _(sp):
            def load_w(w):
                if w:
                    sp.wait_ge(w_hi_ready, w)
                    sp.wait_ge(w_lo_ready, w)
                at = 0
                for c, n in W_TILES[w][2]:
                    sp.dma_start(w_raw[:, :, at:at + n], w_k[:, :, c:c + n]).then_inc(w_in_sem, 16)
                    at += n

            def load_rows(r):
                if r >= len(x_rooms):
                    sp.wait_ge(x_ready, r - len(x_rooms) + 1)
                sp.dma_start(x_raw[r], mem_t[r] if r < MT else x_t[r - MT]).then_inc(x_in[r], 16)

            def load_wm(w):
                if w >= 2:
                    sp.wait_ge(j_done, w - 1)
                sp.dma_start(wm_raw[:, w % 2], wm_k[:, :, P * w:P * w + P]).then_inc(wm_in[w % 2], 16)

            load_rows(0)
            load_rows(1)
            sp.dma_start(gm_row, g_mem.broadcast_to([P, D])).then_inc(rows_in[0], 16)
            load_rows(2)
            sp.dma_start(g_row, g_in.broadcast_to([P, D])).then_inc(rows_in[1], 16)
            load_rows(3)
            load_wm(0)
            load_rows(4)
            load_w(0)
            load_rows(5)
            load_wm(1)
            for r in range(6, MT + NT):
                load_rows(r)
            load_w(1)
            load_wm(2)
            load_wm(3)
            sp.wait_ge(x_ready, len(x_rooms) - 1)
            sp.dma_start(dist[:, :], dist_tab).then_inc(consts_in, 16)
            next_w = 2

            def load_ahead(w):
                nonlocal next_w
                while next_w < min(w, N_W):
                    load_w(next_w)
                    next_w += 1

            def store_mixed(p, g):
                cut = slice(HALF * g, HALF * g + HALF)
                sp.wait_ge(og_ready, 2 * p + g + 1)
                sp.dma_start(mixed_dram[p][:, cut], gates(p)[:, cut]).then_inc(og_stored[g], 16)

            def load_wo(n):
                if n == WO_ROOMS - 1:
                    sp.wait_ge(w_hi_ready, N_W)
                    sp.wait_ge(w_lo_ready, N_W)
                if n >= WO_ROOMS:
                    sp.wait_ge(wo_hi_ready, n - WO_ROOMS + 1)
                    sp.wait_ge(wo_lo_ready[(n - WO_ROOMS) % 2], (n - WO_ROOMS) // 2 + 1)
                sp.dma_start(wo_raw[n % WO_ROOMS], wo_k[PAIRS[n][2]]).then_inc(wo_in[n % WO_ROOMS], 16)

            def load_residual(t):
                sp.dma_start(y_rows[t], x_t[t]).then_inc(xr_in[t], 16)

            def load_mixed(t):
                sp.wait_ge(og_stored[t // EARLY], 16 * (NP - 1))
                if t >= 2:
                    sp.wait_ge(mix_hi_ready, t - 1)
                    sp.wait_ge(mix_lo_ready, t - 1)
                sp.dma_start(mixed[t % 2], mixed_dram[:, :, P * t:P * t + P].rearrange("q p t -> p q t")) \
                    .then_inc(mixed_in[t % 2], 16)

            load_ahead(PRE_W + 3)
            for s in range(STEPS):
                p, i = pair_of_step(s)
                if i == 0 and PAIRS[p][0] == "A":
                    for a in range(2):
                        sp.wait_ge(biased[a], s)
                        if PAIRS[p - 1][0] == "M":
                            sp.wait_ge(biased[1 - a], s)
                        sp.dma_start(bias[:, a, :], a_tab[2 * PAIRS[p][1] + a]).then_inc(bias_in, 16)
                if s == (NP - 1) * NT:
                    load_wo(2)
                if s >= 1 and i % 4 == 0 and s <= (NP - 1) * NT:
                    store_mixed((s - 1) // NT, (s - 1) % NT // 4)
                load_ahead(coming(s) + 3)
                last = s - (STEPS - NT)
                if last == -NT:
                    load_wo(0)
                    load_wo(1)
                if last >= 0:
                    for n in wo_of_step(s):
                        if WO_ROOMS <= n + WO_ROOMS - 1 < NP:
                            load_wo(n + WO_ROOMS - 1)
                if last == 4:
                    for b in range(2):
                        sp.wait_ge(wo_lo_ready[b], NP // 2)
                        load_mixed(b)
                    for g in range(2):
                        sp.wait_ge(og_stored[g], 16 * (NP - 1))
                    load_residual(0)
                    sp.wait_ge(pv_done, CHUNK0[STEPS - 2 * NT])
                    load_residual(1)
                    for a in range(2):
                        sp.wait_ge(biased[a], s)
                    load_residual(2)
                    sp.wait_ge(mask_ready, len(IDX_TILES))
                    load_residual(3)
                if last == 5:
                    for a in range(2):
                        sp.wait_ge(biased[a], s)
                    sp.dma_start(gf_row, g_final.unsqueeze(0).broadcast_to([P, D])).then_inc(gf_in, 16)
                if last == 6:
                    load_mixed(2)
            assert next_w == N_W
            for parity in range(2):
                for a in range(2):
                    sp.wait_ge(pt_done[a], CHUNK0[STEPS - 1 + parity])
                    load_residual(EARLY + 2 * parity + a)
                load_mixed(3 + parity)
            load_mixed(5)
            load_mixed(6)
            for t in range(NT):
                if t == EARLY:
                    load_mixed(7)
                sp.wait_ge(y_final, t + 1)
                sp.dma_start(out_t[t], y_rows[t]).then_inc(stored, 16)
            sp.wait_ge(stored, 16 * NT)

        @block.gpsimd
        def _(pool):
            pool.memset(ident[:, :], 0.0).then_inc(ident_ready, 1)
            pool.wait_ge(ident_ready, 1)
            pool.affine_select(out=ident[:, :], in_=ident[:, :], compare_op=ALU.not_equal, fill=1.0, base=0,
                               pattern=[[-1, P]], channel_multiplier=1).then_inc(ident_ready, 1)

            def split_lo(w):
                pool.wait_ge(w_hi_ready, w + 1)
                n = width(w)
                pool.tensor_tensor(w_hl[:, w % 2, 1, :, 0:n], w_raw[:, :, 0:n],
                                   w_hl[:, w % 2, 0, :, 0:n].bitcast(F32), ALU.subtract).then_inc(w_lo_ready, 1)

            pool.iota(eight[:, :], pattern=[[1, 8]], base=0, channel_multiplier=0,
                      allow_small_or_imprecise_dtypes=True).then_inc(eight_ready, 1)
            for w in range(PRE_W):
                split_lo(w)
            for n, i in enumerate(IDX_TILES):
                if n in (2, 4):
                    split_lo(PRE_W + n // 2 - 1)
                pool.wait_ge(reach_ready, n + 1)
                diagonal = x_slice(i)[:, P * i:P * (i + 1)]
                pool.affine_select(out=diagonal, in_=diagonal, compare_op=ALU.is_ge, fill=-BIG, base=0,
                                   pattern=[[-1, P]], channel_multiplier=1).then_inc(idx_masked, 1)
            pool.wait_ge(consts_in, 16)
            next_w = PRE_W + 2
            masks = 0
            for s in range(STEPS):
                p, i = pair_of_step(s)
                if i == 0 and 1 <= p <= len(IDX_TILES):
                    pool.wait_ge(spoiled, p)
                    pool.partition_all_reduce(failed[:, :], tk[:, 5:6], P, bass.bass_isa.ReduceOp.add)\
                        .then_inc(spoiled_any, 1)
                    t = IDX_TILES[p - 1]
                    n = P * (t + 1)
                    pool.wait_ge(topk_done, p)
                    pool.tensor_scalar(x_slice(t), picked[:, n - 1::-1], -2e38, BIG,
                                       ALU.is_le, ALU.mult).then_inc(half_mask, 1)
                    masks += 1
                    pool.wait_ge(half_mask, masks)
                    pool.tensor_tensor(x_slice(t), x_slice(t), dist_slice(t), ALU.add).then_inc(mask_ready, 1)
                while next_w < min(coming(s) + 2, N_W):
                    split_lo(next_w)
                    next_w += 1
                for n in [n for n in wo_of_step(s) if n % 2 == 0]:
                    pool.wait_ge(wo_hi_ready, n + 1)
                    pool.tensor_tensor(wo_lo[:, n, :], wo_raw[n % WO_ROOMS],
                                       wo_hi[:, n, :].bitcast(F32), ALU.subtract).then_inc(wo_lo_ready[0], 1)
            def mix_lo(t):
                pool.wait_ge(mix_hi_ready, t + 1)
                pool.tensor_tensor(w_hl[:, t % 2, 1, 0:NP - 1, :], mixed[t % 2],
                                   w_hl[:, t % 2, 0, 0:NP - 1, :].bitcast(F32), ALU.subtract).then_inc(mix_lo_ready, 1)

            def last_lo(t):
                pool.wait_ge(last_hi_ready, t + 1)
                pool.tensor_tensor(w_hl[:, t % 2, 1, NP - 1, :], gates(NP - 1)[:, P * t:P * t + P],
                                   w_hl[:, t % 2, 0, NP - 1, :].bitcast(F32), ALU.subtract).then_inc(last_lo_ready, 1)

            mix_lo(0)
            mix_lo(1)
            last_lo(0)
            last_lo(1)
            for t in range(2, NT):
                mix_lo(t)
                last_lo(t)

        @block.scalar
        def _(act):

            def square_sum(r):
                act.wait_ge(x_in[r], 16)
                if r >= 2:
                    act.wait_ge(squares_ready, r // 2)
                act.activation(gate[:, :], x_raw[r], ACT.Square,
                               accum_out=stat[:, 0, r:r + 1]).then_inc(squares_ready, 1)

            def root(n):
                a, b = 2 * n, 2 * n + 2
                act.wait_ge(var_ready, n + 1)
                act.activation(stat[:, 2, a:b], stat[:, 1, a:b], ACT.Sqrt).then_inc(root_ready, 1)

            def split_hi(w):
                act.wait_ge(w_in_sem, 16 * sum(len(W_TILES[q][2]) for q in range(w + 1)))
                if w >= 2:
                    act.wait_ge(j_done, projected(w - 2))
                n = width(w)
                act.activation(w_hl[:, w % 2, 0, :, 0:n], w_raw[:, :, 0:n], ACT.Copy).then_inc(w_hi_ready, 1)

            def evacuate(m):
                kind, w, b = uses[m]
                bank = bank_of(m)
                act.wait_ge(j_done, m + 1)
                cut = slice(HALF * b, HALF * b + HALF)
                if kind == "mem":
                    dst = k_m[:, w, :] if w < 2 else vmT[:, w - 2, :]
                    last = act.activation(dst, bank[:, 0:N_MEM], ACT.Copy)
                elif kind == "memturn":
                    act.wait_ge(x_ready, V_M_ROOM + 1)
                    last = act.activation(v_m, bank[:, :].rearrange("p (t f) -> p t f", t=MT), ACT.Copy)
                elif kind == "wturn":
                    last = act.activation(w_i[:, :, :], bank[:, 0:NT * H_I].rearrange("p (t c) -> p t c", t=NT),
                                          ACT.Copy, scale=float(H_I) ** -0.5)
                else:
                    what, p, _ = W_TILES[w]
                    if what in ("v", "kvB") and b == 1:
                        act.wait_ge(v_turned, v_turns_before(p, 1))
                    if what in ("kIwI", "kvB"):
                        act.activation(kk_b[0:DH, 0, cut], bank[0:DH, :], ACT.Copy)
                        n = H_I if what == "kIwI" else DH
                        dst = w_iT[b] if what == "kIwI" else vT[0:n, :]
                        last = act.activation(dst, bank[DH:DH + n, :], ACT.Copy)
                    elif what == "qI":
                        act.activation(q_i[0:DH, 2 * p, cut], bank[0:DH, :], ACT.Copy, scale=DH ** -0.5)
                        last = act.activation(q_i[DH:P, 2 * p + 1, cut], bank[DH:P, :], ACT.Copy, scale=DH ** -0.5)
                    elif what == "k":
                        for a in range(2):
                            rows = slice(DH * a, DH * a + DH)
                            last = act.activation(qk[rows, K_SLOT[p % 2] + a, cut], bank[rows, :], ACT.Copy)
                    elif what == "v":
                        last = act.activation(vT[:, :], bank[:, :], ACT.Copy)
                    elif what == "q" and PAIRS[p][0] == "M":
                        last = act.activation(q_m[:, cut], bank[:, :], ACT.Copy, scale=query_scale(p, 0))
                    elif what == "q":
                        for a in range(2):
                            rows = slice(DH * a, DH * a + DH)
                            last = act.activation(qk[rows, a, cut], bank[rows, :], ACT.Copy, scale=query_scale(p, a))
                    else:
                        if p == NP - 1:
                            act.wait_ge(pv_done, CHUNK0[(NP - 3) * NT])
                        elif p >= 1:
                            act.wait_ge(og_stored[b], 16 * p)
                        last = act.activation(gates(p)[:, cut], bank[:, :], ACT.Copy)
                last.then_inc(j_free, 1)
                if m in key_uses:
                    act.wait_ge(j_free, m + 1)
                    if W_TILES[w][0] == "k":
                        slot = K_SLOT[W_TILES[w][1] % 2]
                        act.activation(qk[DH:P, slot, cut], qk[0:DH, slot, cut].bitcast(F32), ACT.Copy)
                        last = act.activation(qk[0:DH, slot + 1, cut], qk[DH:P, slot + 1, cut].bitcast(F32), ACT.Copy)
                    else:
                        last = act.activation(kk_b[DH:P, 0, cut], kk_b[0:DH, 0, cut].bitcast(F32), ACT.Copy)
                    last.then_inc(k_copied, 1)
                if kind == "w" and W_TILES[w][0] == "gate" and b == 1:
                    act.wait_ge(j_free, m + 1)
                    act.activation(gates(W_TILES[w][1]), gates(W_TILES[w][1]), ACT.Silu).then_inc(gate_ready, 1)

            def high(u):
                r, b = u // 2, u % 2
                act.wait_ge(turned, u + 1)
                src = turn_banks[u % 6].rearrange("p (k t) -> p k t", k=4)
                if r < MT:
                    dst = memT[:, 4 * b:4 * b + 4, P * r:P * r + P]
                else:
                    dst = h_hi[:, 4 * b:4 * b + 4, P * (r - MT):P * (r - MT) + P]
                act.activation(dst, src, ACT.Copy).then_inc(hi_ready, 1)

            def highs(r):
                high(2 * r)
                high(2 * r + 1)

            uses_emptied = [0]

            def evacuate_next():
                evacuate(uses_emptied[0])
                uses_emptied[0] += 1

            square_sum(0)
            root(0)
            square_sum(2)
            root(1)
            square_sum(4)
            highs(0)
            highs(1)
            root(2)
            highs(2)
            split_hi(0)
            square_sum(6)
            evacuate_next()
            highs(3)
            root(3)
            evacuate_next()
            highs(4)
            square_sum(8)
            evacuate_next()
            highs(5)
            root(4)
            evacuate_next()
            highs(6)
            evacuate_next()
            highs(7)
            split_hi(1)
            evacuate_next()
            highs(8)
            evacuate_next()
            highs(9)
            evacuate_next()
            split_hi(2)
            evacuate_next()
            evacuate_next()
            for w in range(2, W_OF["q", 0]):
                split_hi(w + 1)
                evacuate_next()
                evacuate_next()
            m = uses_emptied[0]
            split_hi(PRE_W - 1)
            for u, (i, h) in enumerate(IDX_UNITS):
                if u % PRE_PAIR_AT == 0:
                    evacuate(m)
                    m += 1
                if u in SPLIT_AT:
                    split_hi(SPLIT_AT[u])
                act.wait_ge(idx_scored, u + 1)
                if u >= 4:
                    act.wait_ge(idx_added, u - 3)
                n = P * (i + 1)
                act.activation(relu[u % 4][:, 0:n], s_ps[u % 2][:, 0:n], ACT.Relu).then_inc(relu_ready, 1)
            def mix_hi(t):
                act.wait_ge(mixed_in[t % 2], 16 * (t // 2 + 1))
                if t >= 2:
                    act.wait_ge(out_done, 2 * (t - 1))
                act.activation(w_hl[:, t % 2, 0, 0:NP - 1, :], mixed[t % 2], ACT.Copy).then_inc(mix_hi_ready, 1)

            def last_hi(t):
                act.wait_ge(og_ready, 2 * (NP - 1) + t // EARLY + 1)
                act.activation(w_hl[:, t % 2, 0, NP - 1, :], gates(NP - 1)[:, P * t:P * t + P],
                               ACT.Copy).then_inc(last_hi_ready, 1)

            next_w = PRE_W + 2

            def copy_probT(s, c):
                g = CHUNK0[s] + c
                act.wait_ge(pt_done[0], g + 1)
                if g >= 2:
                    act.wait_ge(pv_done, g - 1)
                n = len(chunks(s)[c])
                act.activation(probT[:, g % 2, 0, 0:n, :], pt_ps[0][:, 0:n, :], ACT.Copy).then_inc(pt_ready[0], 1)

            def keep_values(p, b):
                act.wait_ge(v_turned, v_turns_before(p, b) + 1)
                n = P if PAIRS[p][0] == "A" else DH
                dst = v_sb[:, p % 2, 4 * b:4 * b + 4, :] if n == P else v_b[:, 4 * b:4 * b + 4, :]
                act.activation(dst, pt_ps[0][:, :, 0:n], ACT.Copy).then_inc(v_kept, 1)

            def exponent(s, a):
                p, i = pair_of_step(s)
                n = P * key_tiles(s)
                act.wait_ge(biased[a], s + 1)
                act.activation(prob[:, a, s % 2, 0:n], prob[:, a, s % 2, 0:n], ACT.Exp, scale=-1.0,
                               bias=nmax[:, a, s % 2:s % 2 + 1],
                               accum_out=lsum[:, p % 2, i, a:a + 1]).then_inc(prob_ready[a], 1)

            for s in range(STEPS + 1):
                if s >= 1:
                    copy_probT(s - 1, 0)
                if s < STEPS:
                    exponent(s, 0)
                    exponent(s, 1)
                if s >= 1 and len(chunks(s - 1)) == 2:
                    copy_probT(s - 1, 1)
                if s < STEPS:
                    if v_turn_of_step(s):
                        keep_values(*v_turn_of_step(s))
                    while next_w < min(coming(s) + 2, N_W):
                        split_hi(next_w)
                        next_w += 1
                    if projection_of_step(s):
                        evacuate(m)
                        m += 1
                    for n in wo_of_step(s):
                        act.wait_ge(wo_in[n % WO_ROOMS], 16 * (n // WO_ROOMS + 1))
                        act.wait_ge(j_done, projected(N_W - 1))
                        act.activation(wo_hi[:, n, :], wo_raw[n % WO_ROOMS], ACT.Copy).then_inc(wo_hi_ready, 1)
                if s == STEPS - 4:
                    act.wait_ge(j_done, projected(N_W - 1))
                    mix_hi(0)
                    mix_hi(1)
                if s == STEPS - 3:
                    last_hi(0)
                    last_hi(1)
                if s in (STEPS - 2, STEPS - 1):
                    mix_hi(s - STEPS + 4)
                    last_hi(s - STEPS + 4)
            assert m == len(uses)

            def square_row(t):
                act.wait_ge(y_added, 2 * t + 2)
                if t >= 1:
                    act.wait_ge(ysq_ready, t)
                act.activation(sq_junk, y_rows[t], ACT.Square, accum_out=stat[:, 0, t:t + 1]).then_inc(ysq_ready, 1)

            def y_root(n, a, b):
                act.wait_ge(yvar_ready, n + 1)
                act.activation(stat[:, 2, a:b], stat[:, 1, a:b], ACT.Sqrt).then_inc(yroot_ready, 1)

            for t in range(NT):
                if t + 4 < EARLY + 2 or t >= EARLY and t + 2 < NT:
                    ahead = t + 4 if t < EARLY else t + 2
                    mix_hi(ahead)
                    last_hi(ahead)
                square_row(t)
                if t >= EARLY - 1:
                    y_root(t - EARLY + 1, 0 if t < EARLY else t, t + 1)

        @block.vector
        def _(dve):
            chain = [0]

            def link(ins):
                chain[0] += 1
                ins.then_inc(dve_seq, 1)
                dve.wait_ge(dve_seq, chain[0])

            def variance(a, b, ready):
                dve.tensor_scalar(stat[:, 1, a:b], stat[:, 0, a:b], 1.0 / D, EPS, ALU.mult, ALU.add).then_inc(ready, 1)

            def inverse_root(a, b):
                v, r, y, t = (stat[:, n, a:b] for n in range(1, 5))
                link(dve.reciprocal(y, r))
                link(dve.tensor_tensor(t, y, y, ALU.mult))
                link(dve.tensor_tensor(t, t, v, ALU.mult))
                link(dve.tensor_scalar(t, t, -0.5, 1.5, ALU.mult, ALU.add))
                link(dve.tensor_tensor(y, y, t, ALU.mult))

            scaled = [0]

            def scale_tile(r):
                if scaled[0] >= 2:
                    dve.wait_ge(turned, 2 * (scaled[0] - 1))
                dve.scalar_tensor_tensor(out=x_scaled[r % 2], in0=x_raw[r], scalar=stat[:, 3, r:r + 1],
                                         in1=(gm_row if r < MT else g_row), op0=ALU.mult,
                                         op1=ALU.mult).then_inc(x_ready, 1)
                scaled[0] += 1

            def low(u):
                r, b = u // 2, u % 2
                dve.wait_ge(hi_ready, u + 1)
                at = (slice(None), slice(4 * b, 4 * b + 4), slice(P * (r - MT), P * (r - MT) + P))
                dve.tensor_tensor(h_lo[at], turn_banks[u % 6].rearrange("p (k t) -> p k t", k=4),
                                  h_hi[at].bitcast(F32), ALU.subtract).then_inc(lo_ready, 1)

            junk = v_b[:, :, :].rearrange("p t f -> p (t f)")

            def square_sum(r):
                dve.wait_ge(x_in[r], 16)
                partial = stat[:, 4, r:r + 1]
                link(dve.tensor_tensor_reduce(junk, x_raw[r][:, 0:HALF], x_raw[r][:, 0:HALF], 1.0, 0.0,
                                              ALU.mult, ALU.add, partial))
                link(dve.tensor_tensor_reduce(junk, x_raw[r][:, HALF:D], x_raw[r][:, HALF:D], 1.0, 0.0,
                                              ALU.mult, ALU.add, stat[:, 0, r:r + 1]))
                link(dve.tensor_tensor(stat[:, 0, r:r + 1], stat[:, 0, r:r + 1], partial, ALU.add))

            def norms(n):
                square_sum(2 * n + 1)
                dve.wait_ge(squares_ready, n + 1)
                variance(2 * n, 2 * n + 2, var_ready)
                dve.wait_ge(root_ready, n + 1)
                inverse_root(2 * n, 2 * n + 2)

            def lows(r):
                low(2 * r)
                low(2 * r + 1)

            norms(0)
            dve.wait_ge(rows_in[0], 16)
            scale_tile(0)
            scale_tile(1)
            norms(1)
            dve.wait_ge(rows_in[1], 16)
            scale_tile(2)
            scale_tile(3)
            norms(2)
            for r in range(2, MT + NT - 2):
                lows(r)
                scale_tile(r + 2)
                if r in (3, 5):
                    norms((r + 3) // 2)
            lows(MT + NT - 2)
            lows(MT + NT - 1)

            def split_low(m):
                _, w, b = uses[m]
                bank = bank_of(m)
                what, p, _ = W_TILES[w]
                cut = slice(HALF * b, HALF * b + HALF)
                dve.wait_ge(j_free, m + 1)

                def part(dst, rows, hi, scale=1.0):
                    return dve.scalar_tensor_tensor(out=dst, in0=bank[rows, :], scalar=scale, in1=hi.bitcast(F32),
                                                    op0=ALU.mult, op1=ALU.subtract)

                lower, upper = slice(0, DH), slice(DH, P)
                if what in ("kIwI", "kvB"):
                    part(kk_b[lower, 1, cut], lower, kk_b[lower, 0, cut])
                    last = part(kk_b[upper, 1, cut], lower, kk_b[lower, 0, cut])
                elif what == "k":
                    slot = K_SLOT[p % 2]
                    part(qk[lower, slot + 2, cut], lower, qk[lower, slot, cut])
                    last = part(qk[upper, slot + 2, cut], upper, qk[upper, slot + 1, cut])
                else:
                    slot = 2 * p if what == "qI" else 0
                    scale = [DH ** -0.5 if what == "qI" else query_scale(p, a) for a in range(2)]
                    part(qk[upper, slot, cut], lower, qk[lower, slot, cut], scale[0])
                    last = part(qk[lower, slot + 1, cut], upper, qk[upper, slot + 1, cut], scale[1])
                last.then_inc(j_split, 1)

            for m in range(use_number["w", W_OF["q", 0], 0]):
                if is_split(m):
                    split_low(m)
            def largest(i):
                dve.tensor_reduce(reach[:, i - FIRST_TOPK:i - FIRST_TOPK + 1], x_slice(i), AX_X, ALU.max,
                                  apply_absolute_value=True).then_inc(reach_ready, 1)

            for u, (i, h) in enumerate(IDX_UNITS):
                if u == 0:
                    dve.wait_ge(j_free, use_number[("wturn", 0, 0)] + 1)
                dve.wait_ge(relu_ready, u + 1)
                n = P * (i + 1)
                wt = w_i[:, i, h:h + 1]
                if h == 0:
                    dve.tensor_scalar(x_slice(i), relu[u % 4][:, 0:n], wt, None, ALU.mult).then_inc(idx_added, 1)
                else:
                    dve.wait_ge(idx_added, u - 1)
                    dve.scalar_tensor_tensor(out=x_slice(i), in0=relu[u % 4][:, 0:n], scalar=wt, in1=x_slice(i),
                                             op0=ALU.mult, op1=ALU.add).then_inc(idx_added, 1)
                if h == H_I - 1 and i % 2 == 1 and i < NT - 1:
                    dve.wait_ge(idx_added, u + 1)
                    largest(i - 1)
                    largest(i)

            def choose(t, slot):
                xs, n = x_slice(t), P * (t + 1)
                level, step, count, extra, flag, late = (tk[:, c:c + 1] for c in (0, 1, 2, 3, 5, 4))
                some = picked[:, 0:n]
                if slot == 0:
                    if t > FIRST_TOPK:
                        dve.wait_ge(mask_ready, t - FIRST_TOPK)
                        dve.wait_ge(spoiled_any, t - FIRST_TOPK)
                    link(dve.tensor_copy(step, reach[:, t - FIRST_TOPK:t - FIRST_TOPK + 1]))
                    link(dve.memset(level, 0.0))
                elif slot <= HALVINGS:
                    if slot == 1 and t == (T - 2 * N_MEM) // P:
                        dve.wait_ge(pv_done, CHUNK0[2 * NT])
                    link(dve.tensor_scalar(some, xs, level, None, ALU.is_ge, ALU.add, accum_out=count))
                    link(dve.tensor_scalar(step, step, 0.5, None, ALU.mult))
                    link(dve.tensor_scalar(count, count, float(TOPK), 0.5, ALU.is_ge, ALU.subtract))
                    link(dve.tensor_scalar(count, count, 2.0, None, ALU.mult))
                    link(dve.scalar_tensor_tensor(out=level, in0=step, scalar=count, in1=level,
                                                  op0=ALU.mult, op1=ALU.add))
                elif slot == HALVINGS + 1:
                    link(dve.scalar_tensor_tensor(out=level, in0=step, scalar=-1.01, in1=level,
                                                  op0=ALU.mult, op1=ALU.add))
                    link(dve.tensor_scalar(some, xs[:, ::-1], level, None, ALU.is_lt, ALU.add, accum_out=count))
                    link(dve.tensor_scalar(extra, count, -1.0, float(n - TOPK), ALU.mult, ALU.add))
                elif slot == HALVINGS + 2:
                    link(dve.scalar_tensor_tensor(out=some, in0=some, scalar=NEVER, in1=xs[:, ::-1],
                                                  op0=ALU.mult, op1=ALU.subtract))
                    link(dve.tensor_scalar(late, extra, 7.5, None, ALU.is_gt))
                    dve.scalar_tensor_tensor(out=flag, in0=extra, scalar=-0.5, in1=late,
                                             op0=ALU.is_lt, op1=ALU.add).then_inc(spoiled, 1)
                elif slot == HALVINGS + 3:
                    if t == FIRST_TOPK:
                        dve.wait_ge(eight_ready, 1)
                    link(dve.max(cut8[:, 0, :], some))
                    link(dve.scalar_tensor_tensor(out=cut8[:, 0, :], in0=eight[:, :], scalar=extra,
                                                  in1=cut8[:, 0, :], op0=ALU.is_lt, op1=ALU.mult))
                    link(dve.tensor_scalar(cut8[:, 1, :], eight[:, :], extra, NEVER, ALU.is_ge, ALU.mult))
                    link(dve.tensor_tensor(cut8[:, 2, :], cut8[:, 0, :], cut8[:, 1, :], ALU.add))
                elif slot == HALVINGS + 4:
                    link(dve.match_replace(out=some, in_to_replace=cut8[:, 2, :], in_values=some, imm_value=NEVER))

            def settle(t):
                xs, n = x_slice(t), P * (t + 1)
                dve.wait_ge(spoiled_any, t - FIRST_TOPK + 1)
                rows = dve.value_load(failed[0:1, 0:1], min_val=0, max_val=P)
                with dve.If(rows > 0):
                    with dve.Fori(0, ROUNDS):
                        dve.max(cut8[:, 0, :], xs)
                        dve.drain()
                        dve.match_replace(out=xs, in_to_replace=cut8[:, 0, :], in_values=xs, imm_value=NEVER)
                        dve.drain()
                    dve.tensor_scalar(picked[:, 0:n], xs[:, ::-1], -2e38, NEVER, ALU.is_ge, ALU.mult)
                dve.drain().then_inc(topk_done, 1)

            def choose_slots(p, slots):
                for slot in slots:
                    choose(IDX_TILES[p], slot)

            def add_bias(s, a):
                p, i = pair_of_step(s)
                g = PAIRS[p][0]
                n = P * key_tiles(s)
                dve.wait_ge(scored[a], s + 1)
                if s >= 2:
                    dve.wait_ge(pt_done[a], CHUNK0[s - 1])
                low_out = nmax[:, a, s % 2:s % 2 + 1]
                dst = prob[:, a, s % 2, 0:n]
                if g == "M":
                    dve.tensor_scalar(dst, s_ps[a][:, 0:n], 1.0, 3e38, ALU.mult, ALU.min,
                                      accum_out=low_out).then_inc(biased[a], 1)
                    return
                if g == "A":
                    if i == 0:
                        dve.wait_ge(bias_in, 32 * (p - 1))
                    table, scale = bias[:, a, T - n:T], 1.0
                else:
                    if i == 0:
                        dve.wait_ge(consts_in, 16)
                    if i >= FIRST_TOPK:
                        dve.wait_ge(mask_ready, i - FIRST_TOPK + 1)
                    table, scale = dist_of(i), slope_of(p, a)
                dve.tensor_tensor_reduce(dst, s_ps[a][:, 0:n], table, scale, 3e38, ALU.add, ALU.min,
                                         low_out).then_inc(biased[a], 1)

            def copy_probT(s, c):
                g = CHUNK0[s] + c
                dve.wait_ge(pt_done[1], g + 1)
                if g >= 2:
                    dve.wait_ge(pv_done, g - 1)
                n = len(chunks(s)[c])
                dve.tensor_copy(probT[:, g % 2, 1, 0:n, :], pt_ps[1][:, 0:n, :]).then_inc(pt_ready[1], 1)

            groups = [0]

            def invert_sums(p, g):
                for a in range(2):
                    dve.wait_ge(prob_ready[a], p * NT + 4 * g + 4)
                inverse = lsum[:, p % 2, 4 * g:4 * g + 4, :]
                link(dve.reciprocal(inverse, inverse))
                dve.tensor_copy(linv[:, :, :, :], inverse.unsqueeze(3).broadcast_to([P, 4, 2, DH])).then_inc(linv_ready, 1)
                groups[0] += 1

            def finish_group(p, g):
                dve.wait_ge(gate_ready, sum(w <= W_OF["gate", p] for (what, _), w in W_OF.items() if what == "gate"))
                dve.wait_ge(linv_turned, groups[0])
                cut = slice(HALF * g, HALF * g + HALF)
                dve.tensor_tensor(gates(p)[:, cut], pt_ps[0][:, :, :].rearrange("p a b -> p (a b)"),
                                  gates(p)[:, cut], ALU.mult).then_inc(linv_used, 1)
                dve.wait_ge(linv_used, groups[0])
                dve.wait_ge(pv_done, CHUNK0[p * NT + 4 * g + 4])
                dve.tensor_tensor(gates(p)[:, cut], o_ps[:, :], gates(p)[:, cut], ALU.mult).then_inc(og_ready, 1)

            def add_residual(t, b):
                bank = j_ps[:, :] if t < EARLY else s_ps[t % 2][:, HALF * b:HALF * b + HALF]
                row = y_rows[t][:, HALF * b:HALF * b + HALF]
                dve.wait_ge(out_done, 2 * t + b + 1)
                dve.wait_ge(xr_in[t], 16)
                dve.tensor_tensor(row, bank, row, ALU.add).then_inc(y_added, 1)

            for s in range(STEPS + 1):
                p, i = pair_of_step(s)
                early = EARLY_OUT.get(s, (None, None, None))
                if s == 0:
                    dve.wait_ge(idx_added, len(IDX_UNITS))
                if s < STEPS:
                    if i == 0 and p < len(IDX_TILES):
                        dve.wait_ge(idx_masked, p + 1)
                    add_bias(s, 0)
                    add_bias(s, 1)
                if s >= 1:
                    copy_probT(s - 1, 0)
                if s >= 1 and (s - 1) % 4 == 3:
                    invert_sums(pair_of_step(s - 1)[0], (s - 1) % NT // 4)
                if s == 0:
                    largest(NT - 2)
                    largest(NT - 1)
                if s < STEPS:
                    if i == 0 and 1 <= p <= len(IDX_TILES):
                        settle(IDX_TILES[p - 1])
                    if i >= 1 and p < len(IDX_TILES):
                        choose_slots(p, CHOICE_SLOTS[2 * i - 2])
                if early[0]:
                    add_residual(*early[0])
                if s >= 1 and len(chunks(s - 1)) == 2:
                    copy_probT(s - 1, 1)
                if early[1]:
                    add_residual(*early[1])
                if s >= 1 and (s - 1) % 4 == 3:
                    finish_group(pair_of_step(s - 1)[0], (s - 1) % NT // 4)
                if early[2]:
                    add_residual(*early[2])
                if s < STEPS and projection_of_step(s) and is_split(use_number["w", *projection_of_step(s)]):
                    split_low(use_number["w", *projection_of_step(s)])
                for n in [n for n in wo_of_step(s) if n % 2 == 1]:
                    dve.wait_ge(wo_hi_ready, n + 1)
                    dve.tensor_tensor(wo_lo[:, n, :], wo_raw[n % WO_ROOMS],
                                      wo_hi[:, n, :].bitcast(F32), ALU.subtract).then_inc(wo_lo_ready[1], 1)
                if s < STEPS and i >= 1 and p < len(IDX_TILES):
                    choose_slots(p, CHOICE_SLOTS[2 * i - 1])

            def final_norm(n, a, b):
                dve.wait_ge(ysq_ready, b)
                variance(a, b, yvar_ready)
                dve.wait_ge(yroot_ready, n + 1)
                inverse_root(a, b)
                for t in range(a, b):
                    dve.scalar_tensor_tensor(out=y_rows[t], in0=y_rows[t], scalar=stat[:, 3, t:t + 1], in1=gf_row,
                                             op0=ALU.mult, op1=ALU.mult).then_inc(y_final, 1)

            dve.wait_ge(gf_in, 16)
            final_norm(0, 0, EARLY)
            for t in range(EARLY, NT):
                add_residual(t, 0)
                add_residual(t, 1)
                final_norm(t - EARLY + 1, t, t + 1)

        @block.tensor
        def _(pe):
            pe.wait_ge(ident_ready, 2)

            def turn(u):
                r, b = u // 2, u % 2
                pe.wait_ge(x_ready, r + 1)
                if u >= 6:
                    pe.wait_ge(hi_ready, u - 5)
                if u - 6 >= 2 * MT:
                    pe.wait_ge(lo_ready, u - 5 - 2 * MT)
                for c in range(4):
                    k = 4 * b + c
                    last = pe.transpose(turn_banks[u % 6][:, P * c:P * c + P], x_scaled[r % 2][:, P * k:P * k + P],
                                        ident[:, :])
                last.then_inc(turned, 1)

            m = 0

            def fill(m, ks=range(KD)):
                kind, w, b = uses[m]
                bank = bank_of(m)
                if free_before(m) > 0 and ks[0] == 0:
                    wait_evacuated(pe, free_before(m) - 1)
                if kind == "mem":
                    pe.wait_ge(wm_in[w % 2], 16 * (w // 2 + 1))
                    for k in range(KD):
                        last = pe.matmul(bank[:, 0:N_MEM], wm_raw[:, w % 2, k, :], memT[:, k, :],
                                         start=(k == 0), stop=(k == KD - 1))
                elif kind == "memturn":
                    pe.wait_ge(j_free, m)
                    for t in range(MT):
                        for f in range(2):
                            at = N_MEM * t + P * f
                            last = pe.transpose(bank[:, at:at + P], vmT[:, f, P * t:P * t + P], ident[:, :])
                elif kind == "wturn":
                    pe.wait_ge(j_free, use_number["w", 0, 1] + 1)
                    for t in range(NT):
                        last = pe.transpose(bank[:, H_I * t:H_I * t + H_I],
                                            w_iT[t // 4][:, P * (t % 4):P * (t % 4) + P], ident[0:H_I, 0:H_I])
                else:
                    if ks[0] == 0:
                        pe.wait_ge(w_lo_ready, w + 1)
                    n = width(w)
                    hi, lo = w_hl[:, w % 2, 0], w_hl[:, w % 2, 1]
                    passes = [(hi, h_hi), (hi, h_lo), (lo, h_hi)]
                    for k in ks:
                        for q, (a, c) in enumerate(passes):
                            last = pe.matmul(bank[0:n, :], a[:, k, 0:n], c[:, k, HALF * b:HALF * b + HALF],
                                             start=(k == 0 and q == 0), stop=(k == KD - 1 and q == 2))
                if kind != "w" or ks[-1] == KD - 1:
                    last.then_inc(j_done, 1)

            def turn_tile(r):
                turn(2 * r)
                turn(2 * r + 1)

            uses_filled = [0]

            def fill_next():
                fill(uses_filled[0])
                uses_filled[0] += 1

            turn_tile(0)
            turn_tile(1)
            turn_tile(2)
            pe.wait_ge(hi_ready, 2 * MT)
            for r in range(3, 6):
                fill_next()
                turn_tile(r)
            fill_next()
            turn_tile(6)
            fill_next()
            turn_tile(7)
            pe.wait_ge(lo_ready, NT)
            fill_next()
            turn_tile(8)
            fill_next()
            turn_tile(9)
            pe.wait_ge(lo_ready, 2 * NT)
            while uses[uses_filled[0]] != ("w", *PRE_PAIR_HALVES[0]):
                fill_next()
            m = uses_filled[0]

            def product(bank, q, k_hi, k_lo, a, i):
                rows = slice(DH * a, DH * a + DH)
                tile = slice(P * i, P * i + P)
                for c in range(0, P * (i + 1), HALF):
                    keys = slice(c, min(c + HALF, P * (i + 1)))
                    pe.matmul(bank[:, keys], q[:, tile], k_hi[:, keys], start=True, stop=False)
                    last = pe.matmul(bank[:, keys], q[rows, tile], k_lo[rows, keys], start=False, stop=True)
                return last

            for u, (i, h) in enumerate(IDX_UNITS):
                if u % PRE_PAIR_AT == 0:
                    fill(m)
                    m += 1
                if u == 0:
                    wait_evacuated(pe, use_number["w", W_OF["q", 0], 0] - 1)
                    pe.wait_ge(k_copied, 2)
                if u >= 2:
                    pe.wait_ge(relu_ready, u - 1)
                product(s_ps[u % 2], q_i[:, h, :], kk_i[:, 0, :], kk_i[:, 1, :], h % 2, i).then_inc(idx_scored, 1)

            def scores(s, a):
                p, i = pair_of_step(s)
                g = PAIRS[p][0]
                if i % 4 == 0 and a == 0:
                    wait_evacuated(pe, use_number["w", W_OF["q", p], i // 4])
                    for what in ("k", "kvB"):
                        if (what, p) in W_OF:
                            pe.wait_ge(k_copied, key_uses.index(use_number["w", W_OF[what, p], i // 4]) + 1)
                if a == 0 and s >= 1 and key_tiles(s) > 4 >= key_tiles(s - 1):
                    lent = [m for m, b in enumerate(bank_ids) if b == 3 and steps_of_uses[m - n_pre] < s]
                    wait_evacuated(pe, lent[-1])
                if s == 0:
                    pe.wait_ge(j_free, n_pre)
                    pe.wait_ge(relu_ready, len(IDX_UNITS))
                else:
                    pe.wait_ge(biased[a], s)
                if g == "M":
                    rows = slice(DH * a, DH * a + DH)
                    last = pe.matmul(s_ps[a][:, 0:N_MEM], q_m[rows, P * i:P * i + P], k_m[rows, PAIRS[p][1], :],
                                     start=True, stop=True)
                elif g == "A":
                    slot = K_SLOT[p % 2]
                    last = product(s_ps[a], qk[:, a, :], qk[:, slot + a, :], qk[:, slot + 2, :], a, i)
                else:
                    last = product(s_ps[a], qk[:, a, :], kk_b[:, 0, :], kk_b[:, 1, :], a, i)
                last.then_inc(scored[a], 1)

            def turn_prob(s, c):
                g = CHUNK0[s] + c
                for a in range(2):
                    pe.wait_ge(prob_ready[a], s + 1)
                    if g >= 1:
                        pe.wait_ge(pt_ready[a], g)
                    if a == 0 and s // 4 >= 1:
                        pe.wait_ge(linv_used, s // 4)
                    if a == 0 and c == 0 and v_turn_of_step(s):
                        pe.wait_ge(v_kept, v_turns_before(*v_turn_of_step(s)) + 1)
                    for n, k in enumerate(chunks(s)[c]):
                        last = pe.transpose(pt_ps[a][:, n, :], prob[:, a, s % 2, P * k:P * k + P], ident[:, :])
                    last.then_inc(pt_done[a], 1)

            def values(s, c):
                p, i = pair_of_step(s)
                g = CHUNK0[s] + c
                pr, j = PAIRS[p][0], PAIRS[p][1]
                for a in range(2):
                    pe.wait_ge(pt_ready[a], g + 1)
                if i % 4 == 0 and c == 0 and (p, i // 4) in V_TURNS:
                    pe.wait_ge(v_kept, v_turns_before(p, i // 4) + 1)
                if i % 4 == 0 and c == 0 and s >= 4:
                    pe.wait_ge(og_ready, s // 4)
                at = slice(P * (i % 4), P * (i % 4) + P)
                nk = key_tiles(s)
                for n, k in enumerate(chunks(s)[c]):
                    for a in range(2):
                        if pr == "A":
                            v = v_sb[:, p % 2, k, DH * a:DH * a + DH]
                        elif pr == "B":
                            v = v_b[:, k, :]
                        else:
                            v = v_m[:, k, P * j + DH * a:P * j + DH * a + DH]
                        last = pe.matmul(o_ps[DH * a:DH * a + DH, at], v, probT[:, g % 2, a, n, :],
                                         start=(k == 0), stop=(k == nk - 1))
                last.then_inc(pv_done, 1)

            def turn_values(s):
                p, b = v_turn_of_step(s)
                pe.wait_ge(j_free, use_number["w", *projection_of_step(s - 1)] + 1)
                pe.wait_ge(pt_ready[0], CHUNK0[s])
                if s // 4 >= 1:
                    pe.wait_ge(linv_used, s // 4)
                n = P if PAIRS[p][0] == "A" else DH
                for c in range(4):
                    last = pe.transpose(pt_ps[0][:, c, 0:n], vT[0:n, P * c:P * c + P], ident[0:n, 0:n])
                last.then_inc(v_turned, 1)

            def turn_sums(s):
                p, i = pair_of_step(s)
                pe.wait_ge(linv_ready, s // 4 + 1)
                pe.wait_ge(pt_ready[0], CHUNK0[s + 1])
                for c in range(4):
                    last = pe.transpose(pt_ps[0][:, c, :], linv[:, c, :, :].rearrange("p a f -> p (a f)"), ident[:, :])
                last.then_inc(linv_turned, 1)

            def project_out(t, b):
                if (t, b) == (0, 0):
                    wait_evacuated(pe, len(uses) - 1)
                    pe.wait_ge(wo_hi_ready, NP)
                    for half in range(2):
                        pe.wait_ge(wo_lo_ready[half], NP // 2)
                elif t < EARLY:
                    pe.wait_ge(y_added, 2 * t + b)
                elif t < EARLY + 2:
                    pe.wait_ge(biased[t % 2], STEPS)
                else:
                    pe.wait_ge(y_added, 2 * (t - 2) + b + 1)
                if b == 0:
                    pe.wait_ge(mix_lo_ready, t + 1)
                    pe.wait_ge(last_lo_ready, t + 1)
                hi, lo = w_hl[:, t % 2, 0], w_hl[:, t % 2, 1]
                passes = [(hi, wo_hi), (hi, wo_lo), (lo, wo_hi)]
                cut = slice(HALF * b, HALF * b + HALF)
                bank = j_ps[:, :] if t < EARLY else s_ps[t % 2][:, cut]
                for p in range(NP):
                    for q, (a, c) in enumerate(passes):
                        last = pe.matmul(bank, a[:, p, :], c[:, p, cut],
                                         start=(p == 0 and q == 0), stop=(p == NP - 1 and q == 2))
                last.then_inc(out_done, 1)

            for s in range(STEPS + 1):
                early = EARLY_OUT.get(s, (None, None, None))
                if s < STEPS:
                    scores(s, 0)
                    scores(s, 1)
                if s >= 1:
                    turn_prob(s - 1, 0)
                two = s >= 1 and len(chunks(s - 1)) == 2
                if s < STEPS and projection_of_step(s):
                    fill(m, range(0, KD // 2 if two else KD))
                if early[0]:
                    project_out(*early[0])
                if s >= 1:
                    values(s - 1, 0)
                if two:
                    turn_prob(s - 1, 1)
                if early[1]:
                    project_out(*early[1])
                if s < STEPS and projection_of_step(s):
                    if two:
                        fill(m, range(KD // 2, KD))
                    m += 1
                if two:
                    values(s - 1, 1)
                if s < STEPS and v_turn_of_step(s):
                    turn_values(s)
                if s >= 1 and (s - 1) % 4 == 3:
                    turn_sums(s - 1)
                if early[2]:
                    project_out(*early[2])
            assert m == len(uses)

            for t in range(EARLY, NT):
                for b in range(2):
                    project_out(t, b)


def distance_table():
    d = np.arange(P)[:, None] + (T - P) - np.arange(T)[None, :]
    return d, np.where(d >= 0, d, BIG).astype(np.float32)


def window_tables():
    d, _ = distance_table()
    count = np.zeros(d.shape)
    for window, dilation in ((128, 1), (512, 4), (2048, 16)):
        count += (d >= 0) & (d % dilation == 0) & (d <= window)
    heads = []
    for h in range(H_A):
        slope = 2.0 ** (-8.0 * (h + 1) / H_A)
        heads.append(np.where(count > 0, slope * d - np.log(np.maximum(count, 1)), BIG))
    return np.stack(heads).astype(np.float32)


_INS = ["x", "mem", "g_in", "g_mem", "w_in", "w_mem_kv", "w_out", "g_final"]


def kernel(**inputs):
    import numpy as _np
    import concourse.bacc as _bacc
    from concourse import mybir as _mybir
    from concourse.bass_utils import run_bass_kernel_spmd as _run

    nc = _bacc.Bacc("TRN2", target_bir_lowering=False, num_devices=1)
    arrays, args = {}, []
    tables = {"dist_tab": distance_table()[1], "a_tab": window_tables()}
    for name in _INS + list(tables):
        a = _np.ascontiguousarray(tables[name] if name in tables else inputs[name])
        arrays[f"in_{name}_dram"] = a
        args.append(nc.dram_tensor(f"in_{name}_dram", a.shape, _mybir.dt.from_np(a.dtype), kind="ExternalInput").ap())
    args.append(nc.dram_tensor("out_0_dram", (1, T, D), F32, kind="ExternalOutput").ap())
    build_program(nc, *args)
    r = _run(nc, [arrays], core_ids=[0])
    return r.results[0]["out_0_dram"]
```
